# Optimizing a Trainium2 kernel written in Bass

```python
import jax
import jax.numpy as jnp
from jax import lax
import numpy as np

D_MODEL = 2048
BATCH = 1
SEQ = 256
DEPTH = 1

GDN_HEAD_DIM = 128
GDN_HEADS = D_MODEL // GDN_HEAD_DIM
GDN_WIDTH = GDN_HEADS * GDN_HEAD_DIM
CONV_K = 4
CHUNK = 64
SWA_HEAD_DIM = 64
SWA_Q_HEADS = D_MODEL // SWA_HEAD_DIM
SWA_KV_HEADS = SWA_Q_HEADS // 8
SWA_Q_WIDTH = SWA_Q_HEADS * SWA_HEAD_DIM
SWA_KV_WIDTH = SWA_KV_HEADS * SWA_HEAD_DIM
WINDOW = 128
N_BRANCH = 2
D_FF = 4 * D_MODEL
PROJ_SIZES = (3 * GDN_WIDTH, GDN_WIDTH, GDN_HEADS, GDN_HEADS, SWA_Q_WIDTH, SWA_KV_WIDTH, SWA_KV_WIDTH, N_BRANCH * D_MODEL)
D_IN = 3 * GDN_WIDTH + GDN_WIDTH + 2 * GDN_HEADS + SWA_Q_WIDTH + 2 * SWA_KV_WIDTH + N_BRANCH * D_MODEL
NORM_EPS = 1e-6

kernel_name = "hybrid_gdn_swa_gated_parallel_trunk"

def rms_norm(x, gain):
    xf = x.astype(jnp.float32)
    y = xf * lax.rsqrt(jnp.mean(xf * xf, axis=-1, keepdims=True) + NORM_EPS)
    return (y * gain.astype(jnp.float32)).astype(x.dtype)

def l2_normalize(x):
    xf = x.astype(jnp.float32)
    return xf * lax.rsqrt(jnp.sum(xf * xf, axis=-1, keepdims=True) + NORM_EPS)

def causal_depthwise_conv(x, w):
    return lax.conv_general_dilated(
        x, w[:, None, :].astype(x.dtype), window_strides=(1,), padding=[(w.shape[0] - 1, 0)],
        dimension_numbers=("NWC", "WIO", "NWC"), feature_group_count=x.shape[-1])

def alibi_slopes(n_heads):
    return 2.0 ** (-8.0 * jnp.arange(1, n_heads + 1, dtype=jnp.float32) / n_heads)

def gated_delta_rule(q, k, v, g, beta):
    B, T, H, Dk = q.shape
    Dv = v.shape[-1]
    N = T // CHUNK
    f32 = jnp.float32

    def to_chunks(t):
        return t.astype(f32).reshape(B, N, CHUNK, H, -1).transpose(0, 3, 1, 2, 4)

    q = to_chunks(q) * (Dk ** -0.5)
    k = to_chunks(k)
    v = to_chunks(v)
    g = to_chunks(g[..., None])[..., 0]
    beta = to_chunks(beta[..., None])
    decay = jnp.cumsum(g, axis=-1)
    idx = jnp.arange(CHUNK)
    causal = idx[:, None] >= idx[None, :]
    strict = idx[:, None] > idx[None, :]
    gamma = jnp.exp(jnp.where(causal, decay[..., :, None] - decay[..., None, :], -jnp.inf))
    k_beta = k * beta
    a_low = jnp.where(strict, jnp.einsum("bhnid,bhnjd->bhnij", k_beta, k) * gamma, 0.0)
    rhs = jnp.concatenate([v * beta, k_beta * jnp.exp(decay)[..., None]], axis=-1)
    sol = lax.linalg.triangular_solve(a_low + jnp.eye(CHUNK, dtype=f32), rhs,
                                      left_side=True, lower=True, unit_diagonal=True)
    u, w = sol[..., :Dv], sol[..., Dv:]
    qk = jnp.einsum("bhnid,bhnjd->bhnij", q, k) * gamma
    q_dec = q * jnp.exp(decay)[..., None]
    k_dec = k * jnp.exp(decay[..., -1:] - decay)[..., None]
    chunk_decay = jnp.exp(decay[..., -1])

    def step(state, inp):
        qk_n, q_n, w_n, u_n, k_n, d_n = inp
        v_new = u_n - jnp.einsum("bhcd,bhde->bhce", w_n, state)
        o_n = jnp.einsum("bhcd,bhde->bhce", q_n, state) + jnp.einsum("bhij,bhje->bhie", qk_n, v_new)
        state = state * d_n[..., None, None] + jnp.einsum("bhcd,bhce->bhde", k_n, v_new)
        return state, o_n

    xs = tuple(jnp.moveaxis(t, 2, 0) for t in (qk, q_dec, w, u, k_dec, chunk_decay))
    _, o = lax.scan(step, jnp.zeros((B, H, Dk, Dv), f32), xs)
    return o.transpose(1, 0, 3, 2, 4).reshape(B, T, H, Dv)

def gdn_branch(qkv, z, b_logit, a_logit, conv_w, a_log, dt_bias, norm_g):
    B, T, _ = qkv.shape
    f32 = jnp.float32
    qkv_c = jax.nn.silu(causal_depthwise_conv(qkv, conv_w))
    q, k, v = jnp.split(qkv_c, 3, axis=-1)

    def heads(t):
        return t.reshape(B, T, GDN_HEADS, GDN_HEAD_DIM)

    q = l2_normalize(heads(q))
    k = l2_normalize(heads(k))
    beta = jax.nn.sigmoid(b_logit.astype(f32))
    g = -jnp.exp(a_log.astype(f32)) * jax.nn.softplus(a_logit.astype(f32) + dt_bias.astype(f32))
    o = gated_delta_rule(q, k, heads(v), g, beta)
    o = rms_norm(o, norm_g) * jax.nn.silu(heads(z).astype(f32))
    return o.reshape(B, T, GDN_WIDTH).astype(qkv.dtype)

def sliding_window_gqa(q, k, v, sinks):
    B, T, _ = q.shape
    NB = T // WINDOW
    G = SWA_Q_HEADS // SWA_KV_HEADS
    f32 = jnp.float32
    qb = q.reshape(B, NB, WINDOW, SWA_KV_HEADS, G, SWA_HEAD_DIM)

    def band(t):
        tb = t.reshape(B, NB, WINDOW, SWA_KV_HEADS, SWA_HEAD_DIM)
        prev = jnp.pad(tb, ((0, 0), (1, 0), (0, 0), (0, 0), (0, 0)))[:, :-1]
        return jnp.concatenate([prev, tb], axis=2)

    kb, vb = band(k), band(v)
    scores = jnp.einsum("bnqkgd,bnskd->bnkgqs", qb, kb).astype(f32) * (SWA_HEAD_DIM ** -0.5)
    qi = jnp.arange(WINDOW)[:, None]
    sj = jnp.arange(2 * WINDOW)[None, :]
    dist = qi + WINDOW - sj
    in_window = (dist >= 0) & (dist < WINDOW)
    after_start = (jnp.arange(NB)[:, None, None] > 0) | (sj >= WINDOW)[None]
    valid = in_window[None] & after_start
    slopes = alibi_slopes(SWA_Q_HEADS).reshape(SWA_KV_HEADS, G)
    bias = -slopes[:, :, None, None] * dist.astype(f32)
    scores = jnp.where(valid[None, :, None, None], scores + bias, -jnp.inf)
    sink = sinks.astype(f32).reshape(SWA_KV_HEADS, G)[:, :, None, None]
    m = jnp.maximum(scores.max(axis=-1, keepdims=True), sink)
    p = jnp.exp(scores - m)
    probs = (p / (p.sum(axis=-1, keepdims=True) + jnp.exp(sink - m))).astype(v.dtype)
    o = jnp.einsum("bnkgqs,bnskd->bnqkgd", probs, vb)
    return o.reshape(B, T, SWA_Q_WIDTH)

def setup_inputs(seed: int = 0) -> dict:
    key = jax.random.key(seed)
    ks = jax.random.split(key, 16)
    f32 = jnp.float32
    nrm = lambda k, shape, scale: jax.random.normal(k, shape, f32) * scale
    dt = jnp.exp(jax.random.uniform(ks[5], (DEPTH, GDN_HEADS), f32, np.log(1e-3), np.log(1e-1)))
    return {
        "x": jax.random.normal(ks[0], (BATCH, SEQ, D_MODEL), f32),
        "norm1_g": 1.0 + nrm(ks[1], (DEPTH, D_MODEL), 0.02),
        "w_in": nrm(ks[2], (DEPTH, D_MODEL, D_IN), D_MODEL ** -0.5),
        "conv_w": nrm(ks[3], (DEPTH, CONV_K, 3 * GDN_WIDTH), CONV_K ** -0.5),
        "a_log": jnp.log(jax.random.uniform(ks[4], (DEPTH, GDN_HEADS), f32, 1.0, 16.0)),
        "dt_bias": dt + jnp.log(-jnp.expm1(-dt)),
        "gdn_norm_g": 1.0 + nrm(ks[6], (DEPTH, GDN_HEAD_DIM), 0.02),
        "attn_sinks": nrm(ks[7], (DEPTH, SWA_Q_HEADS), 0.5),
        "w_branch_gdn": nrm(ks[8], (DEPTH, GDN_WIDTH, D_MODEL), GDN_WIDTH ** -0.5),
        "w_branch_swa": nrm(ks[9], (DEPTH, SWA_Q_WIDTH, D_MODEL), SWA_Q_WIDTH ** -0.5),
        "w_out": nrm(ks[10], (DEPTH, D_MODEL, D_MODEL), D_MODEL ** -0.5),
        "norm2_g": 1.0 + nrm(ks[11], (DEPTH, D_MODEL), 0.02),
        "w_ff_up": nrm(ks[12], (DEPTH, D_MODEL, D_FF), D_MODEL ** -0.5),
        "w_ff_down": nrm(ks[13], (DEPTH, D_FF, D_MODEL), D_FF ** -0.5),
        "final_norm_g": 1.0 + nrm(ks[14], (D_MODEL,), 0.02),
    }

def reference(x, norm1_g, w_in, conv_w, a_log, dt_bias, gdn_norm_g, attn_sinks, w_branch_gdn,
              w_branch_swa, w_out, norm2_g, w_ff_up, w_ff_down, final_norm_g):
    split_points = [int(s) for s in np.cumsum(PROJ_SIZES)[:-1]]
    for l in range(DEPTH):
        h = rms_norm(x, norm1_g[l])
        proj = h @ w_in[l]
        qkv_g, z, b_logit, a_logit, q_s, k_s, v_s, gate_logits = jnp.split(proj, split_points, axis=-1)
        y_gdn = gdn_branch(qkv_g, z, b_logit, a_logit, conv_w[l], a_log[l], dt_bias[l],
                           gdn_norm_g[l]) @ w_branch_gdn[l]
        y_swa = sliding_window_gqa(q_s, k_s, v_s, attn_sinks[l]) @ w_branch_swa[l]
        gates = jax.nn.sigmoid(gate_logits.astype(jnp.float32)).astype(x.dtype)
        g_gdn, g_swa = jnp.split(gates, N_BRANCH, axis=-1)
        x = x + (g_gdn * y_gdn + g_swa * y_swa) @ w_out[l]
        h = rms_norm(x, norm2_g[l])
        x = x + jnp.square(jax.nn.relu(h @ w_ff_up[l])) @ w_ff_down[l]
    return rms_norm(x, final_norm_g)


_drawn_inputs = setup_inputs


def setup_inputs(seed=0):
    import zlib

    import numpy as np

    out = dict(_drawn_inputs(seed))
    spreads = {}
    factors = {'norm1_g': 4.347,
     'gdn_norm_g': 8.0,
     'attn_sinks': 142.203,
     'norm2_g': 12.745,
     'final_norm_g': 21.416}
    for name, (base, spread) in spreads.items():
        noise = np.random.default_rng([zlib.crc32(name.encode()), seed]).standard_normal(out[name].shape)
        drawn = base * np.exp(spread * noise) if base else spread * noise
        out[name] = jnp.asarray(drawn.astype(out[name].dtype))
    for name, factor in factors.items():
        out[name] = (out[name] * factor).astype(out[name].dtype)
    return out
```

```python
from contextlib import ExitStack

import concourse.bass as bass
from concourse import mybir
import numpy as np

ALU = mybir.AluOpType
ACT = mybir.ActivationFunctionType
F32 = mybir.dt.float32
F32R = mybir.dt.float32r
AX_X = mybir.AxisListType.X

P = 128
T = 256
NT = T // P
D = 2048
KT = D // P
DFF = 4 * D
NB = 512
HG = 4
NG = 4
C = 64
NCH = T // C
U = NT * HG
HQ = 8
CK = 2
CPO = KT // CK
RING = 4
AHEAD = 3
EPS = 1e-6
NEG = -3.0e38
LEVELS = 5

OUT_SWA = 4 * NG
OUT_MIX1 = OUT_SWA + 5
OUT_MIX2 = OUT_MIX1 + 8
OUT_WO = OUT_MIX2 + 8
OUT_FF = OUT_WO + 4
FF_UP, FF_DOWN = 8, 4
CH_FF = OUT_FF * CPO
CH_HALF = FF_UP * CPO + FF_DOWN * 2 * CPO
N_CHUNKS = CH_FF + 2 * CH_HALF

G, BETA, BHALF, K_OUT, Q_OUT, K_DEC, DCOL, CHDEC0, CHDEC1 = range(9)
M_AT, M_X, M_U, M_V, M_B0, M_B1, M_KQ = range(7)
ITEM_K, ITEM_Q, ITEM_V, ITEM_Z = range(4)
FRONT = {ITEM_K: 0, ITEM_Q: 5, ITEM_V: 22, ITEM_Z: 35}
TAPS = {ITEM_K: (0, 0, 0), ITEM_Q: (6, 6, 6), ITEM_V: (23, 26, 29)}
TANH = {ITEM_K: 1, ITEM_Q: 7, ITEM_V: 30}
SILU = {ITEM_K: 2, ITEM_Q: 8, ITEM_V: 31}
BACK = {ITEM_K: 4, ITEM_Q: 12, ITEM_V: 32}
NORM = {ITEM_K: 7, ITEM_Q: 15}
TK, TQ, ROWS, KKQ, INV, QTM, SCAN, OT = 9, 17, 14, 20, 24, 39, 38, 63


def hybrid_trunk(nc, x, weights, w_ba, colp_d, rowp_d, masks_d, dist_d, fgain_d, out):
    with ExitStack() as ctx:
        def sb(name, shape, dt=F32, where=ctx):
            return where.enter_context(nc.sbuf_tensor(name, shape, dt))

        def sem(name):
            return ctx.enter_context(nc.semaphore(name))

        raw = sb("raw", [P, RING, CK * NB])
        w_hi = sb("w_hi", [P, RING, CK * NB], F32R)
        w_lo = sb("w_lo", [P, RING, CK * NB], F32R)
        hT_hi = sb("hT_hi", [P, KT, T], F32R)
        hT_lo = sb("hT_lo", [P, KT, T], F32R)
        xres = sb("xres", [P, NT, D])
        masks = sb("masks_sb", [P, 5 * P + 12 * C])
        colp = sb("colp_sb", [P, 48 * 4 + 2 * KT + 3])
        rowp = sb("rowp_sb", [P, 128])
        stat = sb("stat", [P, 16])
        kT = sb("kT", [P, 4, T])
        vs = sb("vs", [P, NT, 4 * C])

        with ExitStack() as mixers:
            og_hi = sb("og_hi", [P, KT, T], F32R, mixers)
            og_lo = sb("og_lo", [P, KT, T], F32R, mixers)
            with ExitStack() as gdn:
                rawg = sb("rawg", [P, 4, NT, NB], where=gdn)
                cT = sb("cT", [P, HG, T], where=gdn)
                vb = sb("vb", [P, NT, NB], where=gdn)
                kn = sb("kn", [P, NT, NB], where=gdn)
                qn = sb("qn", [P, NT, NB], where=gdn)
                kq = sb("kq", [P, HG, NCH * P], where=gdn)
                zs = sb("zs", [P, HG, T], where=gdn)
                mats = sb("mats", [P, 7, U, C], where=gdn)
                solve = sb("solve", [P, U, 2, C], where=gdn)
                S = sb("S", [P, HG, P], where=gdn)
                sc = sb("sc", [P, 9, NT, 16], where=gdn)
                scg = sb("scg", [P, 9, NT, HG], where=gdn)
                cwg = sb("cwg", [P, 3, HG, 4], where=gdn)
                rg = sb("rg", [P, 3, 8], where=gdn)
            with ExitStack() as swa:
                os_hi = sb("os_hi", [P, KT, T], F32R, swa)
                os_lo = sb("os_lo", [P, KT, T], F32R, swa)
                gb = sb("gb", [P, NT, NB], where=swa)
                qfix = sb("qfix", [P, NT, NB], where=swa)
                qTs = sb("qTs", [P, 4, T], where=swa)
                kfix = sb("kfix", [P, T], where=swa)
                vfix = sb("vfix", [P, NT, C], where=swa)
                dist = sb("dist_sb", [P, 3 * P], where=swa)
                sbuf_s = sb("sbuf_s", [P, 2, 3 * P], where=swa)
                prob = sb("prob", [P, 2, 3 * P], where=swa)
                probT = sb("probT", [P, 2, 3 * P], where=swa)
                oS = sb("oS", [P, NT, NB], where=swa)
                slf = sb("slf", [P, 2, HQ], where=swa)
                r3 = sb("r3", [P, HQ, 3], where=swa)
                negm = sb("negm", [P, HQ, 2], where=swa)
                lsum = sb("lsum", [P, HQ, 2], where=swa)
                esink = sb("esink", [P, HQ, 2], where=swa)
        with ExitStack() as mlp:
            act_hi = sb("act_hi", [P, 32, T], F32R, mlp)
            act_lo = sb("act_lo", [P, 32, T], F32R, mlp)
            rbuf = sb("rbuf", [P, 2, NT, NB], where=mlp)
            nat = sb("nat", [P, NT, D], where=mlp)
            fgain = sb("fgain_sb", [P, D], where=mlp)

        acc = ctx.enter_context(nc.psum_tensor("acc", [P, 2, NT, NB], F32))
        J = ctx.enter_context(nc.psum_tensor("J", [P, 4, NB], F32))

        ident, tri, tri_swap, chunk_ones, ones = (masks[:, i * P:(i + 1) * P] for i in range(5))
        (tri64, eye64, low, upi, up, nlow1, nup1, *up_level) = (
            masks[:, 5 * P + i * C:5 * P + (i + 1) * C] for i in range(12))
        conv_w = colp[:, 0:192].rearrange("p (k n c) -> p k n c", k=3, c=4)
        gain_cols = (colp[:, 192:192 + KT], None, colp[:, 192 + KT:192 + 2 * KT])
        gdn_gain = colp[:, 224:225]
        chunk_sel = colp[:, 225:227]
        dt_bias, a_log = rowp[:, 0:32], rowp[:, 32:64]
        slopes, sinks = rowp[:, 64:96], rowp[:, 96:128]
        RH = mats[:, M_B0].rearrange("p u c -> p (u c)")
        VO = mats[:, M_V].rearrange("p u c -> p (u c)")
        qn3, kn3, vb3 = (a[:].rearrange("p t (h e) -> p (t h) e", h=HG) for a in (qn, kn, vb))
        cT2 = cT[:].rearrange("p h t -> p (h t)")
        cTu = cT[:].rearrange("p h (t e) -> p (h t) e", t=NT)
        nat1 = rawg[:].rearrange("p a t n -> p (a t n)").rearrange("p (t d) -> p t d", t=NT)
        w_ba_sb = zs[:].rearrange("p h t -> p (h t)")[:, 0:512]
        ba = vb[:].rearrange("p t n -> p (t n)")
        kdup = rawg[:, 0]

        def mat(i):
            return mats[:, i]

        def scu(kind):
            return scg[:, kind].rearrange("p t h -> p (t h)")

        def wide(a, n):
            return a.unsqueeze(2).broadcast_to([a.shape[0], a.shape[1], n])

        def over(a, n):
            return a.unsqueeze(1).broadcast_to([a.shape[0], n, a.shape[1]])

        step_begun = sem("step_begun")
        params_in, x_in, raw_in = sem("params_in"), sem("x_in"), [sem(f"raw_in{i}") for i in range(RING)]
        hi_ready, lo_ready, chunk_used = sem("hi_ready"), sem("lo_ready"), sem("chunk_used")
        ssq_x, r_x, pool_x, nat_a, nat_d = (sem(n) for n in ("ssq_x", "r_x", "pool_x", "nat_a", "nat_d"))
        turn_T, turn_hi, turn_lo = sem("turn_T"), sem("turn_hi"), sem("turn_lo")
        ba_split, ba_done, ba_link, ba_act = (sem(n) for n in ("ba_split", "ba_done", "ba_link", "ba_act"))
        g_ready, decay_done, sc_ready = sem("g_ready"), sem("decay_done"), sem("sc_ready")
        rawg_a, rawg_d, par_ready = sem("rawg_a"), sem("rawg_d"), sem("par_ready")
        front_T, conv_0, conv_tap, tanh_done, silu_done, back_T = (
            sem(n) for n in ("front_T", "conv_0", "conv_tap", "tanh_done", "silu_done", "back_T"))
        vb_done, nsq_done, nssq_done, nr_link, nr_done, norm_done = (
            sem(n) for n in ("vb_done", "nsq_done", "nssq_done", "nr_link", "nr_done", "norm_done"))
        qk_T, kq_a, kq_d = sem("qk_T"), sem("kq_a"), sem("kq_d")
        rows_rhs, rows_done, arg_done, exp_done, mask_done = (
            sem(n) for n in ("rows_rhs", "rows_done", "arg_done", "exp_done", "mask_done"))
        kkq_done, at_ready, x0_link, xu_link, x0_ready, u0_ready, bt_ready, vpass, vcopy, zpass, inv_done = (
            sem(n) for n in ("kkq_done", "at_ready", "x0_link", "xu_link", "x0_ready", "u0_ready", "bt_ready", "vpass", "vcopy", "zpass", "inv_done"))
        qt_done, qt_copied, kdec_done = sem("qt_done"), sem("qt_copied"), sem("kdec_done")
        s_ready, p1_done, rh_done, p2_done, vo_done, o_done, p3_done = (
            sem(n) for n in ("s_ready", "p1_done", "rh_done", "p2_done", "vo_done", "o_done", "p3_done"))
        osq_done, ossq_done, or_done, on_done, o_T, og_f, og_hi_done, og_lo_done = (
            sem(n) for n in ("osq_done", "ossq_done", "or_done", "on_done", "o_T", "og_f", "og_hi_done", "og_lo_done"))
        kv_a, kv_d, kv_T, kT_done, sq_a, sq_d = (sem(n) for n in ("kv_a", "kv_d", "kv_T", "kT_done", "sq_a", "sq_d"))
        dist_in, qfix_done, fix_done, q_T, qT_a, qT_d = (
            sem(n) for n in ("dist_in", "qfix_done", "fix_done", "q_T", "qT_a", "qT_d"))
        score_done, bias_done, max_link, negm_done, exps_done = (
            sem(n) for n in ("score_done", "bias_done", "max_link", "negm_done", "exps_done"))
        p_T, pT_copied, pv_done, l_link, oS_done = (sem(n) for n in ("p_T", "pT_copied", "pv_done", "l_link", "oS_done"))
        oS_T, os_hi_done, os_lo_done = sem("oS_T"), sem("os_hi_done"), sem("os_lo_done")
        gate_done, merged, merge_link = sem("gate_done"), sem("merged"), sem("merge_link")
        relu_done, relu_sq, up_T, act_hi_done, act_lo_done = (
            sem(n) for n in ("relu_done", "relu_sq", "up_T", "act_hi_done", "act_lo_done"))
        x_added, y_ready, y_out = sem("x_added"), sem("y_ready"), sem("y_out")

        block = ctx.enter_context(nc.Block())

        @block.sync
        def _(sp):
            sp.dma_start(xres[:], x).then_inc(x_in, 16)
            for dst, src in ((masks, masks_d), (colp, colp_d), (rowp, rowp_d)):
                sp.dma_start(dst[:], src).then_inc(params_in, 16)
            sp.dma_start(w_ba_sb, w_ba).then_inc(params_in, 16)
            for i in range(RING):
                sp.dma_start(raw[:, i], weights[i]).then_inc(raw_in[i], 16)

            def stream(a, b):
                with sp.Fori(a, b) as q:
                    for i in range(RING):
                        sp.wait_ge(lo_ready, RING * q + (i - RING + 1))
                        sp.dma_start(raw[:, i], weights[bass.ds(RING * q + i, 1)].rearrange(
                            "a p n -> p (a n)")).then_inc(raw_in[i], 16)

            first_swa = OUT_MIX1 * CPO // RING
            stream(1, first_swa)
            sp.wait_ge(og_lo_done, NG)
            sp.dma_start(dist[:], dist_d).then_inc(dist_in, 16)
            reload_x = (OUT_WO * CPO) // RING
            stream(first_swa, reload_x + 1)
            sp.wait_ge(turn_T, 2 * CPO)
            sp.dma_start(xres[:], x).then_inc(x_in, 16)
            stream(reload_x + 1, OUT_FF * CPO // RING)
            sp.dma_start(fgain[:], fgain_d).then_inc(dist_in, 16)
            stream(OUT_FF * CPO // RING, N_CHUNKS // RING)
            for t in range(NT):
                sp.wait_ge(y_ready, t + 1)
                sp.dma_start(out[t], nat[:, t]).then_inc(y_out, 16)
            sp.wait_ge(y_out, 16 * NT)

        @block.tensor
        def _(pe):
            mm, tr = nc.tensor.matmul, nc.tensor.transpose

            def output(c0, par, aT_hi, aT_lo, free, jobs=None, nch=CPO, h0=0):
                for c in range(nch):
                    pe.wait_ge(lo_ready, c0 + (c + 1))
                    if c == 0:
                        for s_free, v in free:
                            if not isinstance(v, int) or v > 0:
                                pe.wait_ge(s_free, v)
                    for k in range(CK):
                        kt = c * CK + k
                        w = slice(k * NB, (k + 1) * NB)
                        for t in range(NT):
                            tok = slice(t * P, (t + 1) * P)
                            o = acc[:, par, t]
                            mm(o, aT_hi[:, kt, tok], w_hi[:, c % RING, w], start=(c == 0 and k == 0), stop=False)
                            mm(o, aT_hi[:, kt, tok], w_lo[:, c % RING, w], start=False, stop=False)
                            last = mm(o, aT_lo[:, kt, tok], w_hi[:, c % RING, w], start=False,
                                      stop=(c == nch - 1 and k == CK - 1))
                        if k == CK - 1:
                            last.then_inc(chunk_used, 1)
                        if jobs:
                            jobs(h0 + c * CK + k)

            def turn(k, src):
                for i in range(CPO):
                    if 8 * k + i >= 4:
                        pe.wait_ge(turn_lo, 8 * k + i - 3)
                    for kk in range(2):
                        for t in range(NT):
                            kt = 2 * i + kk
                            ins = tr(J[:, i % 4, kk * T + t * P:kk * T + (t + 1) * P],
                                     src[:, t, kt * P:(kt + 1) * P], ident)
                    ins.then_inc(turn_T, 1)

            def turn_group(src, b0, sem_, dst_cols=None):
                for m in range(HG):
                    for t in range(NT):
                        ins = tr(J[:, b0 + m // 2, (m % 2) * T + t * P:(m % 2) * T + (t + 1) * P],
                                 src[:, t, m * P:(m + 1) * P], ident)
                ins.then_inc(sem_, 1)

            def gdn_step(h, g):
                for n in range(4):
                    if h == FRONT[n]:
                        pe.wait_ge(rawg_a, 4 * g + (n + 1))
                        if n == ITEM_K:
                            pe.wait_ge(rawg_d, 4 * g + 4)
                        if n == ITEM_Q:
                            pe.wait_ge(silu_done, 4 * g + 1)
                        if n == ITEM_V:
                            pe.wait_ge(at_ready, g + 1)
                        if n == ITEM_Z:
                            pe.wait_ge(vb_done, g + 1)
                        turn_group(rawg[:, n], 0 if n < ITEM_V else 2, front_T)
                for n in (ITEM_K, ITEM_Q, ITEM_V):
                    if h == BACK[n]:
                        pe.wait_ge(silu_done, 4 * g + (n + 1))
                        if n == ITEM_Q:
                            pe.wait_ge(kq_a, 2 * g + 1)
                            pe.wait_ge(kq_d, g + 1)
                        for t in range(NT):
                            for m in range(HG):
                                ins = tr(J[:, 2 + t, m * P:(m + 1) * P], cT[:, m, t * P:(t + 1) * P], ident)
                        ins.then_inc(back_T, 1)
                if h == TK or h == TQ:
                    n = 0 if h == TK else 1
                    pe.wait_ge(norm_done, 2 * g + (n + 1))
                    src = qn if n else kn
                    for t in range(NT):
                        for m in range(HG):
                            ins = tr(J[:, 2 + t, m * P:(m + 1) * P], src[:, t, m * P:(m + 1) * P], ident)
                    ins.then_inc(qk_T, 1)
                if h == ROWS:
                    pe.wait_ge(rows_rhs, 2 * g + 2)
                    pe.wait_ge(silu_done, 4 * g + 2)
                    mm(J[:, 0], chunk_ones, mat(M_B0), start=True, stop=True)
                    mm(J[:, 1], chunk_ones, mat(M_B1), start=True, stop=True).then_inc(rows_done, 1)
                if h == KKQ:
                    pe.wait_ge(kq_a, 2 * g + 2)
                    pe.sem_inc(step_begun, 1)
                    for bank in range(2):
                        for u in range(U):
                            t, hd = divmod(u, HG)
                            for ck in range(2):
                                c = 2 * t + ck
                                kc = kq[:, hd, c * P + ck * C:c * P + ck * C + C]
                                qc = kq[:, hd, c * P + (1 - ck) * C:c * P + (1 - ck) * C + C]
                                ins = mm(J[ck * C:ck * C + C, 2 + bank, u * C:(u + 1) * C], kc,
                                         qc if bank else kc, start=True, stop=True)
                    ins.then_inc(kkq_done, 1)

                def per_chunk(bank, lhs, rhs, done):
                    for u in range(U):
                        for ck in range(2):
                            r = slice(ck * C, ck * C + C)
                            ins = mm(J[r, bank, u * C:(u + 1) * C], lhs[r, u], rhs[r, u], start=True, stop=True)
                    if done is not None:
                        ins.then_inc(done, 1)

                for lv in range(LEVELS):
                    if h == INV + 3 * lv:
                        pe.wait_ge(bt_ready, LEVELS * g + (lv + 1))
                        if lv:
                            pe.wait_ge(inv_done, LEVELS * g + lv)
                        else:
                            pe.wait_ge(x0_ready, g + 1)
                        pe.sem_inc(step_begun, 1)
                        per_chunk(0, mat(M_B0 + lv % 2), mat(M_X), vpass)
                    if h == INV + 3 * lv + 1:
                        pe.wait_ge(vcopy, LEVELS * g + (lv + 1))
                        if lv == 0:
                            pe.wait_ge(u0_ready, 2 * g + 2)
                        pe.sem_inc(step_begun, 1)
                        per_chunk(1, mat(M_U), mat(M_V), None)
                        per_chunk(0, mat(M_V), mat(M_U), zpass)
                if h == QTM:
                    pe.wait_ge(inv_done, LEVELS * (g + 1))
                    pe.wait_ge(silu_done, 4 * g + 4)
                    pe.sem_inc(step_begun, 1)
                    per_chunk(3, mat(M_X), mat(M_KQ), qt_done)
                for c in range(NCH):
                    t, ck = divmod(c, 2)
                    kr = slice(ck * C, ck * C + C)
                    if h == SCAN + 6 * c:
                        pe.wait_ge(s_ready, NCH * g + (c + 1))
                        if c:
                            pe.wait_ge(o_done, NCH * g + c)
                        for hd in range(HG):
                            ins = mm(J[:, 0, hd * P:(hd + 1) * P], kq[:, hd, c * P:(c + 1) * P], S[:, hd],
                                     start=True, stop=True)
                        ins.then_inc(p1_done, 1)
                    if h == SCAN + 6 * c + 2:
                        pe.wait_ge(rh_done, NCH * g + (c + 1))
                        if c == 0:
                            pe.wait_ge(qt_copied, g + 1)
                        for hd in range(HG):
                            ins = mm(J[:, 1, hd * P:(hd + 1) * P], solve[kr, t * HG + hd].rearrange("p a c -> p (a c)"),
                                     RH[kr, hd * P:(hd + 1) * P], start=True, stop=True)
                        ins.then_inc(p2_done, 1)
                    if h == SCAN + 6 * c + 4 and c < NCH - 1:
                        pe.wait_ge(vo_done, NCH * g + (c + 1))
                        if c == 0:
                            pe.wait_ge(kdec_done, g + 1)
                        for hd in range(HG):
                            ins = mm(J[:, 2, hd * P:(hd + 1) * P], kn[kr, t, hd * P:(hd + 1) * P],
                                     VO[kr, hd * P:(hd + 1) * P], start=True, stop=True)
                        ins.then_inc(p3_done, 1)
                if h == OT:
                    pe.wait_ge(on_done, g + 1)
                    turn_group(qn, 0, o_T)

            def swa_step(h, j):
                if h == 1:
                    pe.wait_ge(qfix_done, j + 1)
                    pe.wait_ge(fix_done, j + 1)
                    turn_group(qfix, 0, q_T)
                for s in range(HQ):
                    r = slice((s % 2) * C, (s % 2) * C + C)
                    pb = s % 2
                    if h == 3 + 3 * s:
                        if s == 0:
                            pe.wait_ge(qT_a, j + 1)
                            pe.wait_ge(qT_d, j + 1)
                            pe.wait_ge(fix_done, j + 1)
                        if s >= 2:
                            pe.wait_ge(bias_done, HQ * j + (s - 1))
                        mm(J[:, pb, 0:P], qTs[r, s // 2, 0:P], kfix[r, 0:P], start=True, stop=True)
                        mm(J[:, pb, P:3 * P], qTs[r, s // 2, P:T], kfix[r, 0:T], start=True,
                           stop=True).then_inc(score_done, 1)
                    if h == 6 + 3 * s:
                        pe.wait_ge(exps_done, HQ * j + (s + 1))
                        if s:
                            pe.wait_ge(pT_copied, HQ * j + s)
                        for i in range(3):
                            ins = tr(J[:, 2, i * P:(i + 1) * P], prob[:, pb, i * P:(i + 1) * P], ident)
                        ins.then_inc(p_T, 1)
                    if h == 8 + 3 * s:
                        pe.wait_ge(pT_copied, HQ * j + (s + 1))
                        if s:
                            pe.wait_ge(oS_done, HQ * j + s)
                        o = J[:, 3, (s % 4) * P:(s % 4 + 1) * P]
                        mm(o[:, 0:C], probT[:, pb, 0:P], vfix[:, 0], start=True, stop=True)
                        mm(o[:, C:P], probT[:, pb, P:2 * P], vfix[:, 0], start=True, stop=False)
                        mm(o[:, C:P], probT[:, pb, 2 * P:3 * P], vfix[:, 1], start=False, stop=True).then_inc(pv_done, 1)
                if h == 31:
                    pe.wait_ge(oS_done, HQ * (j + 1))
                    turn_group(oS, 0, oS_T)

            pe.wait_ge(params_in, 64)
            pe.wait_ge(nat_a, 1)
            pe.wait_ge(nat_d, 1)
            turn(0, nat1)
            pe.wait_ge(turn_lo, 8)
            pe.wait_ge(ba_split, 2)
            for t in range(NT):
                tok = slice(t * P, (t + 1) * P)
                for kt in range(KT):
                    w = slice(kt * 32, (kt + 1) * 32)
                    o = J[:, 0, t * 32:(t + 1) * 32]
                    mm(o, hT_hi[:, kt, tok], w_hi[:, 3, w], start=(kt == 0), stop=False)
                    mm(o, hT_hi[:, kt, tok], w_lo[:, 3, w], start=False, stop=False)
                    ins = mm(o, hT_lo[:, kt, tok], w_hi[:, 3, w], start=False, stop=(kt == KT - 1))
            ins.then_inc(ba_done, 1)

            def decay_step(h):
                if h == 10:
                    pe.wait_ge(g_ready, 3)
                    gall = sc[:, G].rearrange("p t h -> p (t h)")
                    for i, lhs in enumerate((tri, chunk_ones, tri_swap)):
                        mm(J[:, 1, i * 32:(i + 1) * 32], lhs, gall, start=True, stop=True)
                    mm(J[:, 1, 96:160], ones, sc[:, CHDEC0:CHDEC1 + 1].rearrange("p c t h -> p (c t h)"),
                       start=True, stop=True).then_inc(decay_done, 1)

            def window(w, jobs):
                for n in range(4):
                    free = [] if isinstance(w, int) and n < 2 else [(rawg_a, 4 * w + (n - 1)), (rawg_d, 4 * w + (n - 1))]
                    output(w * (4 * CPO) + n * CPO, n % 2, hT_hi, hT_lo, free, jobs, h0=16 * n)

            window(0, decay_step)
            with pe.Fori(1, NG) as w:
                window(w, lambda h: gdn_step(h, w - 1))

            def kv_step(h):
                gdn_step(h, NG - 1)
                if h == 66:
                    pe.wait_ge(kv_a, 1)
                    pe.wait_ge(kv_d, 1)
                    for m in range(4):
                        for t in range(NT):
                            ins = tr(J[:, 2 + m // 2, (m % 2) * T + t * P:(m % 2) * T + (t + 1) * P],
                                     kdup[:, t, m * P:(m + 1) * P], ident)
                    ins.then_inc(kv_T, 1)

            free5 = [[(rawg_a, 15), (rawg_d, 15)], [(rawg_a, 16), (rawg_d, 16)], [(kv_a, 1), (kv_d, 1)],
                     [(sq_a, 1), (sq_d, 1)], [(sq_a, 2), (sq_d, 2)]]
            for n in range(5):
                output((OUT_SWA + n) * CPO, n % 2, hT_hi, hT_lo, free5[n], kv_step, h0=16 * n)

            pe.wait_ge(og_hi_done, NG)
            pe.wait_ge(og_lo_done, NG)
            pe.wait_ge(kT_done, 1)
            pe.wait_ge(sq_a, 3)
            pe.wait_ge(sq_d, 3)
            def mix1(j):
                c0 = j * (2 * CPO) + OUT_MIX1 * CPO
                output(c0, 1, hT_hi, hT_lo, [(gate_done, j)], lambda h: swa_step(h, j), h0=0)
                output(c0 + CPO, 0, og_hi, og_lo, [(sq_a, 4), (sq_d, 4), (merged, j)], lambda h: swa_step(h, j), h0=16)
            mix1(0)
            with pe.Fori(1, 4) as j:
                mix1(j)
            pe.wait_ge(os_lo_done, 4)
            with pe.Fori(0, 4) as j:
                c0 = j * (2 * CPO) + OUT_MIX2 * CPO
                output(c0, 1, hT_hi, hT_lo, [(gate_done, j + 4)])
                output(c0 + CPO, 0, os_hi, os_lo, [(merged, j + 4)])

            pe.wait_ge(merged, 8)
            turn(1, xres)
            pe.wait_ge(turn_lo, 16)
            for i in range(4):
                output((OUT_WO + i) * CPO, 1 - i % 2, og_hi, og_lo, [(x_added, i - 1)] if i >= 2 else [(gate_done, 8)])
            pe.wait_ge(nat_a, 2)
            pe.wait_ge(nat_d, 2)
            turn(2, nat)
            pe.wait_ge(turn_lo, 24)

            def up_out(p, c0, prev, free):
                def job(h):
                    if prev is not None and h == 2:
                        pe.wait_ge(relu_sq, prev)
                        if not isinstance(prev, int) or prev > 1:
                            pe.wait_ge(act_lo_done, prev - 1)
                        turn_group(rbuf[:, 1 - p], 2 * (1 - p), up_T)
                output(c0, 1 - p, hT_hi, hT_lo, free, job)

            for hf in range(2):
                c0, r0, x0 = CH_FF + hf * CH_HALF, FF_UP * hf, 4 + 4 * hf
                for p in range(2):
                    up_out(p, c0 + p * CPO, (r0 + p) if p else None, [(x_added, x0 - 1 + p)])
                with pe.Fori(1, FF_UP // 2) as i:
                    for p in range(2):
                        up_out(p, i * (2 * CPO) + (c0 + p * CPO), i * 2 + (r0 + p), [(relu_sq, i * 2 + (r0 + p - 1))])
                cd = c0 + FF_UP * CPO

                def last_T(h):
                    if h == 2:
                        pe.wait_ge(relu_sq, r0 + FF_UP)
                        pe.wait_ge(act_lo_done, r0 + FF_UP - 1)
                        turn_group(rbuf[:, 1], 2, up_T)
                    if h == 27:
                        pe.wait_ge(act_lo_done, r0 + FF_UP)

                pe.wait_ge(act_lo_done, r0 + FF_UP - 1)
                for d in range(FF_DOWN):
                    output(cd + d * 2 * CPO, 1 - d % 2, act_hi, act_lo,
                           [(relu_sq, r0 + 7 + d)] if d < 2 else [(x_added, x0 + d - 1)],
                           last_T if d == 0 else None, nch=2 * CPO)

        @block.scalar
        def _(act):
            A = nc.scalar.activation

            def split(q, k):
                slot, dq = k % RING, k // RING
                if isinstance(q, int) and RING * q + k >= N_CHUNKS:
                    return
                act.wait_ge(raw_in[slot], 16 * (q + (dq + 1)))
                if not isinstance(q, int) or RING * q + k > RING - 1:
                    act.wait_ge(chunk_used, RING * q + (k - RING + 1))
                A(w_hi[:, slot], raw[:, slot], ACT.Copy).then_inc(hi_ready, 1)

            def output(q0, jobs, epilogue, nch=CPO, h0=0):
                for c in range(nch):
                    split(q0, c + AHEAD)
                    for k in range(CK):
                        if jobs:
                            jobs(h0 + c * CK + k)
                epilogue()

            def turn(k):
                dst = og_hi if k == 1 else hT_hi
                for i in range(CPO):
                    act.wait_ge(turn_T, 8 * k + i + 1)
                    if k == 1:
                        A(dst[:, 2 * i:2 * i + 2, :], J[:, i % 4].rearrange("p (a t) -> p a t", a=2), ACT.Copy,
                          scale=0.5).then_inc(turn_hi, 1)
                        continue
                    for kk in range(2):
                        ins = A(dst[:, 2 * i + kk, :], J[:, i % 4, kk * T:(kk + 1) * T], ACT.Copy,
                                scale=gain_cols[k][:, 2 * i + kk:2 * i + kk + 1])
                    ins.then_inc(turn_hi, 1)

            def norm_rows(k, src, dst):
                for t in range(NT):
                    ins = A(dst[:, t], src[:, t], ACT.Square, accum_out=stat[:, t:t + 1])
                ins.then_inc(ssq_x, 1)
                act.wait_ge(r_x, k)
                act.wait_ge(ssq_x, k)
                A(dst[:, 0], src[:, 0], ACT.Copy, scale=stat[:, 2:3]).then_inc(nat_a, 1)

            def gdn_step(h, g):
                if h == FRONT[ITEM_Z]:
                    act.wait_ge(front_T, 4 * g + 4)
                    act.wait_ge(silu_done, 4 * g + 3)
                    for b in range(2):
                        ins = A(zs[:, 2 * b:2 * b + 2].rearrange("p a t -> p (a t)"), J[:, 2 + b], ACT.Tanh, scale=0.5)
                    ins.then_inc(tanh_done, 1)
                for n in (ITEM_K, ITEM_Q, ITEM_V):
                    if h == FRONT[n]:
                        act.wait_ge(front_T, 4 * g + (n + 1))
                        if n == ITEM_K:
                            act.wait_ge(par_ready, g + 1)
                        else:
                            act.wait_ge(back_T, 3 * g + n)
                        b0 = 2 if n == ITEM_V else 0
                        for m in range(HG):
                            ins = A(cT[:, m], J[:, b0 + m // 2, (m % 2) * T:(m % 2 + 1) * T], ACT.Copy,
                                    scale=cwg[:, n, m, 3:4])
                        ins.then_inc(conv_0, 1)
                    if h == TANH[n]:
                        act.wait_ge(conv_tap, 9 * g + 3 * (n + 1))
                        A(zs[:].rearrange("p h t -> p (h t)"), cT2, ACT.Tanh, scale=0.5).then_inc(tanh_done, 1)
                for n, dst, dst3 in ((ITEM_K, kn, kn3), (ITEM_Q, qn, qn3)):
                    if h == BACK[n]:
                        act.wait_ge(back_T, 3 * g + (n + 1))
                        for t in range(NT):
                            ins = A(dst[:, t], J[:, 2 + t], ACT.Square)
                        ins.then_inc(nsq_done, 1)
                    if h == NORM[n]:
                        act.wait_ge(nr_done, 2 * g + (n + 1))
                        for u in range(U):
                            ins = A(dst3[:, u], J[:, 2 + u // HG, (u % HG) * P:(u % HG + 1) * P], ACT.Copy,
                                    scale=rg[:, n, u:u + 1])
                        ins.then_inc(norm_done, 1)
                if h == TK:
                    act.wait_ge(qk_T, 2 * g + 1)
                    dst = kq[:, :, 0:T].rearrange("p h (a c) -> p h a c", a=4)[:, :, 0:4:3]
                    A(dst, J[:, 2].rearrange("p (h a c) -> p h a c", h=HG, a=2), ACT.Copy).then_inc(kq_a, 1)
                if h == TQ:
                    act.wait_ge(qk_T, 2 * g + 2)
                    for t in range(NT):
                        ins = A(kq[:, :, t * T + C:t * T + C + P], J[:, 2 + t].rearrange("p (h t) -> p h t", h=HG), ACT.Copy)
                    ins.then_inc(kq_a, 1)
                if h == ROWS:
                    act.wait_ge(arg_done, g + 1)
                    A(mat(M_X), mat(M_X), ACT.Exp)
                    A(mat(M_U), mat(M_U), ACT.Exp, scale=-1.0)
                    A(mat(M_B0), J[:, 1].rearrange("p (u c) -> p u c", u=U), ACT.Copy).then_inc(exp_done, 1)
                for lv in range(LEVELS):
                    if h == INV + 3 * lv:
                        act.wait_ge(vpass, LEVELS * g + (lv + 1))
                        A(mat(M_V), J[:, 0].rearrange("p (u c) -> p u c", u=U), ACT.Copy).then_inc(vcopy, 1)
                if h == QTM:
                    act.wait_ge(qt_done, g + 1)
                    for ck in range(2):
                        r = slice(ck * C, ck * C + C)
                        ins = A(solve[r, :, 1 - ck], J[r, 3].rearrange("p (u c) -> p u c", u=U), ACT.Copy)
                    ins.then_inc(qt_copied, 1)
                for c in range(NCH):
                    if h == SCAN + 6 * c + 2:
                        act.wait_ge(p2_done, NCH * g + (c + 1))
                        A(VO, J[:, 1], ACT.Copy).then_inc(vo_done, 1)
                if h == SCAN + 21:
                    act.wait_ge(o_done, NCH * (g + 1))
                    A(cT2, qn[:].rearrange("p t n -> p (t n)"), ACT.Square).then_inc(osq_done, 1)
                if h == OT:
                    act.wait_ge(og_f, g + 1)
                    A(og_hi[:, bass.ds(g * HG, HG), :], cT[:], ACT.Copy).then_inc(og_hi_done, 1)

            def swa_step(h, j):
                if h == 0:
                    act.wait_ge(sq_d, 4)
                    act.wait_ge(sq_a, 4)
                    A(qfix[:], xres[:, :, bass.ds(j * NB, NB)], ACT.Copy).then_inc(qfix_done, 1)
                if h == 1:
                    act.wait_ge(q_T, j + 1)
                    A(qTs[:, 0:2], J[:, 0].rearrange("p (a t) -> p a t", a=2), ACT.Copy).then_inc(qT_a, 1)
                for s in range(HQ):
                    pb = s % 2
                    if h == 3 + 3 * s:
                        act.wait_ge(negm_done, HQ * j + (s + 1))
                        if s >= 2:
                            act.wait_ge(p_T, HQ * j + (s - 1))
                        A(prob[:, pb, 0:P], sbuf_s[:, pb, 0:P], ACT.Exp, bias=negm[:, s, 0:1], accum_out=lsum[:, s, 0:1])
                        A(prob[:, pb, P:3 * P], sbuf_s[:, pb, P:3 * P], ACT.Exp, bias=negm[:, s, 1:2],
                          accum_out=lsum[:, s, 1:2])
                        A(esink[:, s], negm[:, s], ACT.Exp, bias=slf[:, 1, s:s + 1]).then_inc(exps_done, 1)
                    if h == 6 + 3 * s:
                        act.wait_ge(p_T, HQ * j + (s + 1))
                        A(probT[:, pb], J[:, 2, 0:3 * P], ACT.Copy).then_inc(pT_copied, 1)
                if h == 31:
                    act.wait_ge(oS_T, j + 1)
                    for b in range(2):
                        ins = A(os_hi[:, bass.ds(j * 4 + 2 * b, 2), :], J[:, b].rearrange("p (a t) -> p a t", a=2), ACT.Copy)
                    ins.then_inc(os_hi_done, 1)

            act.wait_ge(x_in, 16)
            norm_rows(1, xres, nat1)
            act.wait_ge(params_in, 64)
            A(w_hi[:, 3, 0:512], w_ba_sb, ACT.Copy).then_inc(ba_split, 1)
            turn(0)
            for k in range(AHEAD):
                split(0, k)
            act.wait_ge(ba_done, 1)
            tb, e, l, ea = ba[:, 64:96], ba[:, 128:160], ba[:, 160:192], ba[:, 192:224]
            ba3 = ba[:, 0:64].rearrange("p (t b h) -> p t b h", t=NT, b=2)
            act.wait_ge(ba_link, 1)
            A(tb.rearrange("p (t h) -> p t h", t=NT), ba3[:, :, 0], ACT.Tanh, scale=0.5)
            A(ea, a_log, ACT.Exp).then_inc(ba_act, 1)
            act.wait_ge(ba_link, 2)
            A(e, ba[:, 96:128], ACT.Abs).then_inc(ba_act, 1)
            act.wait_ge(ba_act, 2)
            A(e, e, ACT.Exp, scale=-1.0).then_inc(ba_act, 1)
            act.wait_ge(ba_act, 3)
            A(l, e, ACT.Ln, bias=1.0).then_inc(ba_act, 1)

            def decay_step(h):
                if h == 10:
                    act.wait_ge(decay_done, 1)
                    fl = lambda k: sc[:, k].rearrange("p t h -> p (t h)")
                    A(fl(K_OUT), J[:, 1, 0:32], ACT.Exp)
                    A(fl(DCOL), J[:, 1, 0:32], ACT.Copy)
                    A(fl(Q_OUT), J[:, 1, 64:96], ACT.Exp)
                    A(sc[:, CHDEC0:CHDEC1 + 1].rearrange("p c t h -> p (c t h)"), J[:, 1, 96:160], ACT.Exp).then_inc(ba_act, 1)
                    act.wait_ge(ba_link, 6)
                    A(fl(K_DEC), fl(K_DEC), ACT.Exp).then_inc(ba_act, 1)

            def read(q_end, ops):
                def f():
                    act.wait_ge(chunk_used, RING * q_end)
                    ops()
                return f

            def window(q0, jobs):
                for n in range(4):
                    def ops(n=n):
                        A(rawg[:, n, 0], acc[:, n % 2, 0], ACT.Copy).then_inc(rawg_a, 1)
                    output(q0 + n * (CPO // RING), jobs, read(q0 + (n + 1) * (CPO // RING), ops), h0=16 * n)

            window(0, decay_step)
            with act.Fori(1, NG) as w:
                window(w * CPO, lambda h: gdn_step(h, w - 1))

            def kv_step(h):
                gdn_step(h, NG - 1)
                if h == 66:
                    act.wait_ge(kv_T, 1)
                    for b in range(2):
                        ins = A(kT[:, 2 * b:2 * b + 2], J[:, 2 + b].rearrange("p (a t) -> p a t", a=2), ACT.Copy)
                    ins.then_inc(kT_done, 1)

            for n in range(5):
                def ops(n=n):
                    if n == 0:
                        act.wait_ge(front_T, 4 * NG - 3)
                        A(kdup[:, 0].rearrange("p (k d c) -> p k d c", k=4, d=2),
                          acc[:, 0, 0, 0:T].rearrange("p (k c) -> p k c", k=4).unsqueeze(2).broadcast_to([P, 4, 2, C]), ACT.Copy)
                        A(vs[:, 0], acc[:, 0, 0, T:2 * T], ACT.Copy).then_inc(kv_a, 1)
                    else:
                        A(xres[:, 0, (n - 1) * NB:n * NB], acc[:, n % 2, 0], ACT.Copy, scale=0.125).then_inc(sq_a, 1)
                q = (OUT_SWA + n) * (CPO // RING)
                output(q, kv_step, read(q + CPO // RING, ops), h0=16 * n)

            def gate(par, k):
                def ops():
                    if not isinstance(k, int) or k > 0:
                        act.wait_ge(merged, k)
                    for t in range(NT):
                        ins = A(gb[:, t], acc[:, par, t], ACT.Tanh, scale=0.5)
                    ins.then_inc(gate_done, 1)
                return ops

            act.wait_ge(og_lo_done, NG)
            def mix1(j):
                q = j * 4 + OUT_MIX1 * 2
                output(q, lambda h: swa_step(h, j), read(q + 2, gate(1, j)), h0=0)
                output(q + 2, lambda h: swa_step(h, j), lambda: None, h0=16)

            mix1(0)
            with act.Fori(1, 4) as j:
                mix1(j)
            with act.Fori(0, 4) as j:
                q = j * 4 + OUT_MIX2 * 2
                output(q, None, read(q + 2, gate(1, j + 4)))
                output(q + 2, None, lambda: None)
            turn(1)
            with act.Fori(0, 4) as i:
                output(i * 2 + OUT_WO * 2, None, lambda: None)
            act.wait_ge(x_added, 4)
            norm_rows(2, xres, nat)
            turn(2)

            def relu(p, par, k, skip):
                def ops():
                    if not skip:
                        act.wait_ge(up_T, k)
                    for t in range(NT):
                        ins = A(rbuf[:, p, t], acc[:, par, t], ACT.Relu)
                    ins.then_inc(relu_done, 1)
                return ops

            def up_job(b0, kt, cnt):
                def job(h):
                    if h == 2:
                        act.wait_ge(up_T, cnt)
                        for b in range(2):
                            ins = A(act_hi[:, bass.ds(kt + 2 * b, 2), :], J[:, b0 + b].rearrange("p (a t) -> p a t", a=2), ACT.Copy)
                        ins.then_inc(act_hi_done, 1)
                return job

            for hf in range(2):
                q0, r0 = (CH_FF + hf * CH_HALF) // RING, FF_UP * hf
                for p in range(2):
                    output(q0 + 2 * p, up_job(0, 0, r0 + 1) if p else None,
                           read(q0 + 2 * p + 2, relu(p, 1 - p, r0 + p - 1, r0 + p < 2)))
                with act.Fori(1, FF_UP // 2) as i:
                    for p in range(2):
                        q = i * 4 + (q0 + 2 * p)
                        output(q, up_job(2 * (1 - p), i * 8 + 4 * (p - 1), i * 2 + (r0 + p)),
                               read(q + 2, relu(p, 1 - p, i * 2 + (r0 + p - 1), False)))
                qd = q0 + FF_UP * 2
                for n in range(FF_DOWN):
                    output(qd + 4 * n, up_job(2, 28, r0 + FF_UP) if n == 0 else None, lambda: None, nch=2 * CPO)
            act.wait_ge(x_added, 12)
            for t in range(NT):
                ins = A(nat[:, t], xres[:, t], ACT.Square, accum_out=stat[:, t:t + 1])
            ins.then_inc(ssq_x, 1)

        @block.vector
        def _(dve):
            V = nc.vector
            tt, ts, stt = V.tensor_tensor, V.tensor_scalar, V.scalar_tensor_tensor

            def split(q, k):
                slot = k % RING
                if isinstance(q, int) and RING * q + k >= N_CHUNKS:
                    return
                dve.wait_ge(hi_ready, RING * q + (k + 1))
                tt(w_lo[:, slot], raw[:, slot], w_hi[:, slot].bitcast(F32), ALU.subtract).then_inc(lo_ready, 1)

            def output(q0, jobs, epilogue, nch=CPO, h0=0):
                for c in range(nch):
                    split(q0, c + AHEAD)
                    for k in range(CK):
                        if jobs:
                            jobs(h0 + c * CK + k)
                epilogue()

            def turn(k):
                hi, lo = (og_hi, og_lo) if k == 1 else (hT_hi, hT_lo)
                for i in range(CPO):
                    dve.wait_ge(turn_hi, 8 * k + i + 1)
                    for kk in range(2):
                        kt = 2 * i + kk
                        ins = stt(out=lo[:, kt, :], in0=J[:, i % 4, kk * T:(kk + 1) * T],
                                  scalar=0.5 if k == 1 else gain_cols[k][:, kt:kt + 1],
                                  in1=hi[:, kt, :].bitcast(F32), op0=ALU.mult, op1=ALU.subtract)
                    ins.then_inc(turn_lo, 1)

            def gdn_step(h, g):
                if h == 0:
                    dve.wait_ge(sc_ready, 1)
                    dve.wait_ge(ba_act, 6)
                    V.tensor_copy(scg[:].rearrange("p k t h -> p (k t) h"),
                                  sc[:].rearrange("p k t h -> p (k t) h")[:, :, bass.ds(g * HG, HG)])
                    V.tensor_copy(cwg[:], conv_w[:, :, bass.ds(g * HG, HG), :]).then_inc(par_ready, 1)
                if h == FRONT[ITEM_Z] + 1:
                    dve.wait_ge(tanh_done, 4 * g + 4)
                    for b in range(2):
                        zb = zs[:, 2 * b:2 * b + 2].rearrange("p a t -> p (a t)")
                        ins = stt(out=zb, in0=zb, scalar=1.0, in1=J[:, 2 + b], op0=ALU.add, op1=ALU.mult)
                    ins.then_inc(silu_done, 1)
                for i, n, dst in ((0, ITEM_K, kn3), (1, ITEM_Q, qn3)):
                    if h == BACK[n] + 1:
                        dve.wait_ge(nsq_done, 2 * g + (i + 1))
                        V.tensor_reduce(rg[:, i], dst, AX_X, ALU.add).then_inc(nr_link, 1)
                        dve.wait_ge(nr_link, 3 * g + (i + 1))
                        f = (1.0, float(P))[i]
                        ts(rg[:, i], rg[:, i], f, 4 * EPS * f, ALU.mult, ALU.add).then_inc(nssq_done, 1)
                for n in (ITEM_K, ITEM_Q, ITEM_V):
                    for s in (1, 2, 3):
                        if h == TAPS[n][s - 1]:
                            if s == 1:
                                dve.wait_ge(conv_0, 3 * g + (n + 1))
                            else:
                                dve.wait_ge(conv_tap, 9 * g + (3 * n + s - 1))
                            b0 = 2 if n == ITEM_V else 0
                            for m in range(HG):
                                b, o = b0 + m // 2, (m % 2) * T
                                ins = stt(out=cT[:, m, s:T], in0=J[:, b, o:o + T - s], scalar=cwg[:, n, m, 3 - s:4 - s],
                                          in1=cT[:, m, s:T], op0=ALU.mult, op1=ALU.add)
                            ins.then_inc(conv_tap, 1)
                    if h == SILU[n]:
                        dve.wait_ge(tanh_done, 4 * g + (n + 1))
                        stt(out=cT2, in0=zs[:].rearrange("p h t -> p (h t)"), scalar=1.0, in1=cT2, op0=ALU.add,
                            op1=ALU.mult).then_inc(silu_done, 1)
                if h == BACK[ITEM_V] + 1:
                    dve.wait_ge(back_T, 3 * g + 3)
                    for t in range(NT):
                        ins = tt(vb3[:, t * HG:(t + 1) * HG], J[:, 2 + t].rearrange("p (h e) -> p h e", h=HG),
                                 wide(scu(BHALF)[:, t * HG:(t + 1) * HG], P), ALU.mult)
                    ins.then_inc(vb_done, 1)
                if h == ROWS:
                    dve.wait_ge(rows_done, g + 1)
                    tt(mat(M_V), J[:, 0].rearrange("p (u c) -> p u c", u=U), wide(scu(DCOL), C), ALU.subtract).then_inc(x0_link, 1)
                    dve.wait_ge(x0_link, g + 1)
                    ts(mat(M_X), mat(M_V), 0.0, None, ALU.min)
                    ts(mat(M_U), mat(M_V), 0.0, None, ALU.max).then_inc(arg_done, 1)
                if h == TK:
                    dve.wait_ge(qk_T, 2 * g + 1)
                    dst = kq[:, :, T:2 * T].rearrange("p h (a c) -> p h a c", a=4)[:, :, 0:4:3]
                    V.tensor_copy(dst, J[:, 3].rearrange("p (h a c) -> p h a c", h=HG, a=2)).then_inc(kq_d, 1)
                if h == KKQ:
                    dve.wait_ge(kkq_done, g + 1)
                    dve.wait_ge(mask_done, 5 * g + 5)
                    kk, kqp = (J[:, b].rearrange("p (u c) -> p u c", u=U) for b in (2, 3))
                    tt(mat(M_V), kk, mat(M_V), ALU.mult)
                    tt(mat(M_AT), kk, mat(M_B1), ALU.mult)
                    tt(mat(M_KQ), kqp, mat(M_KQ), ALU.mult).then_inc(at_ready, 1)
                if h == KKQ + 1:
                    dve.wait_ge(at_ready, g + 1)
                    tt(mat(M_U), mat(M_AT), over(nup1, U), ALU.mult).then_inc(u0_ready, 1)
                    dve.wait_ge(u0_ready, 2 * g + 1)
                    tt(mat(M_U), mat(M_U), over(eye64, U), ALU.add).then_inc(u0_ready, 1)
                for lv in range(LEVELS):
                    if h == INV + 3 * lv + 1:
                        dve.wait_ge(zpass, LEVELS * g + (lv + 1))
                        tt(mat(M_X), mat(M_X), J[:, 1].rearrange("p (u c) -> p u c", u=U), ALU.subtract)
                        z = J[:, 0].rearrange("p (u c) -> p u c", u=U)
                        if lv < LEVELS - 1:
                            tt(mat(M_U), mat(M_U), z, ALU.subtract).then_inc(inv_done, 1)
                            continue
                        for ck in range(2):
                            r = slice(ck * C, ck * C + C)
                            ins = tt(solve[r, :, ck], mats[r, M_U], z[r], ALU.subtract)
                        ins.then_inc(inv_done, 1)
                        V.memset(S[:], 0.0).then_inc(s_ready, 1)
                for c in range(NCH):
                    t, ck = divmod(c, 2)
                    kr, qr = slice(ck * C, ck * C + C), slice((1 - ck) * C, (2 - ck) * C)
                    if h == SCAN + 6 * c:
                        dve.wait_ge(p1_done, NCH * g + (c + 1))
                        if c == 0:
                            dve.wait_ge(vb_done, g + 1)
                        for hd in range(HG):
                            ins = stt(out=RH[kr, hd * P:(hd + 1) * P], in0=J[kr, 0, hd * P:(hd + 1) * P],
                                      scalar=scg[kr, K_OUT, t, hd:hd + 1], in1=vb[kr, t, hd * P:(hd + 1) * P],
                                      op0=ALU.mult, op1=ALU.add)
                        ins.then_inc(rh_done, 1)
                    if h == SCAN + 6 * c + 2:
                        dve.wait_ge(vo_done, NCH * g + (c + 1))
                        for hd in range(HG):
                            ins = stt(out=qn[qr, t, hd * P:(hd + 1) * P], in0=J[qr, 0, hd * P:(hd + 1) * P],
                                      scalar=scg[qr, Q_OUT, t, hd:hd + 1], in1=VO[qr, hd * P:(hd + 1) * P],
                                      op0=ALU.mult, op1=ALU.add)
                        ins.then_inc(o_done, 1)
                    if h == SCAN + 6 * c + 4 and c < NCH - 1:
                        dve.wait_ge(p3_done, 3 * g + (c + 1))
                        dve.wait_ge(s_ready, NCH * g + (c + 1))
                        for hd in range(HG):
                            ins = stt(out=S[:, hd], in0=S[:, hd], scalar=scg[:, CHDEC0 + ck, t, hd:hd + 1],
                                      in1=J[:, 2, hd * P:(hd + 1) * P], op0=ALU.mult, op1=ALU.add)
                        ins.then_inc(s_ready, 1)
                if h == SCAN + 22:
                    dve.wait_ge(osq_done, g + 1)
                    V.tensor_reduce(rg[:, 2], cT2.rearrange("p (u e) -> p u e", u=U), AX_X, ALU.add).then_inc(nr_link, 1)
                    dve.wait_ge(nr_link, 3 * g + 3)
                    ts(rg[:, 2], rg[:, 2], 4.0 / P, 4 * EPS, ALU.mult, ALU.add).then_inc(ossq_done, 1)
                if h == SCAN + 23:
                    dve.wait_ge(or_done, g + 1)
                    tt(qn3, qn3, wide(rg[:, 2], P), ALU.mult).then_inc(on_done, 1)
                if h == OT:
                    dve.wait_ge(o_T, g + 1)
                    for b in range(2):
                        src = J[:, b].rearrange("p (u a c) -> p u a c", u=4, a=2)
                        zz = zs[:, 2 * b:2 * b + 2].rearrange("p h (t a c) -> p (h t) a c", t=NT, a=2)
                        oo = cT[:, 2 * b:2 * b + 2].rearrange("p h (t a c) -> p (h t) a c", t=NT, a=2)
                        for a in range(2):
                            ins = stt(out=oo[:, :, a], in0=src[:, :, 1 - a], scalar=gdn_gain, in1=zz[:, :, a],
                                      op0=ALU.mult, op1=ALU.mult)
                    ins.then_inc(og_f, 1)
                    dve.wait_ge(og_hi_done, g + 1)
                    dve.wait_ge(og_f, g + 1)
                    tt(og_lo[:, bass.ds(g * HG, HG), :], cT[:], og_hi[:, bass.ds(g * HG, HG), :].bitcast(F32),
                       ALU.subtract).then_inc(og_lo_done, 1)

            def swa_step(h, j):
                if h == 0:
                    dve.wait_ge(kT_done, 1)
                    dve.wait_ge(kv_d, 1)
                    V.tensor_copy(kfix[:], kT[:, bass.ds(j, 1), :].rearrange("p a t -> p (a t)"))
                    V.tensor_copy(vfix[:], vs[:, :, bass.ds(j * C, C)])
                    V.tensor_copy(slf[:], rowp[:, 64:128].rearrange("p (a n) -> p a n", a=2)[:, :, bass.ds(j * HQ, HQ)]).then_inc(fix_done, 1)
                if h == 1:
                    dve.wait_ge(q_T, j + 1)
                    V.tensor_copy(qTs[:, 2:4], J[:, 1].rearrange("p (a t) -> p a t", a=2)).then_inc(qT_d, 1)
                for s in range(HQ):
                    pb = s % 2
                    if h == 3 + 3 * s:
                        dve.wait_ge(score_done, HQ * j + (s + 1))
                        if s == 0:
                            dve.wait_ge(fix_done, j + 1)
                            dve.wait_ge(dist_in, 16)
                        if s >= 2:
                            dve.wait_ge(exps_done, HQ * j + (s - 1))
                        stt(out=sbuf_s[:, pb], in0=dist[:], scalar=slf[:, 0, s:s + 1], in1=J[:, pb, 0:3 * P],
                            op0=ALU.mult, op1=ALU.add).then_inc(bias_done, 1)
                        dve.wait_ge(bias_done, HQ * j + (s + 1))
                        V.tensor_reduce(r3[:, s], sbuf_s[:, pb].rearrange("p (a k) -> p a k", a=3), AX_X, ALU.max).then_inc(max_link, 1)
                        dve.wait_ge(max_link, j * (2 * HQ) + (2 * s + 1))
                        tt(r3[:, s, 1:2], r3[:, s, 1:2], r3[:, s, 2:3], ALU.max).then_inc(max_link, 1)
                        dve.wait_ge(max_link, j * (2 * HQ) + (2 * s + 2))
                        ts(negm[:, s], r3[:, s, 0:2], slf[:, 1, s:s + 1], -1.0, ALU.max, ALU.mult).then_inc(negm_done, 1)
                    if h == 8 + 3 * s:
                        dve.wait_ge(pv_done, HQ * j + (s + 1))
                        tt(lsum[:, s], lsum[:, s], esink[:, s], ALU.add).then_inc(l_link, 1)
                        dve.wait_ge(l_link, j * (2 * HQ) + (2 * s + 1))
                        V.reciprocal(lsum[:, s], lsum[:, s]).then_inc(l_link, 1)
                        dve.wait_ge(l_link, j * (2 * HQ) + (2 * s + 2))
                        tt(oS[:, :, s * C:(s + 1) * C], J[:, 3, (s % 4) * P:(s % 4 + 1) * P].rearrange("p (t c) -> p t c", t=NT),
                           wide(lsum[:, s], C), ALU.mult).then_inc(oS_done, 1)
                if h == 31:
                    dve.wait_ge(os_hi_done, j + 1)
                    for b in range(2):
                        ins = tt(os_lo[:, bass.ds(j * 4 + 2 * b, 2), :], J[:, b].rearrange("p (a t) -> p a t", a=2),
                                 os_hi[:, bass.ds(j * 4 + 2 * b, 2), :].bitcast(F32), ALU.subtract)
                    ins.then_inc(os_lo_done, 1)

            dve.wait_ge(x_in, 16)
            dve.wait_ge(r_x, 1)
            ts(nat1[:, 1], xres[:, 1], stat[:, 3:4], None, ALU.mult).then_inc(nat_d, 1)
            dve.wait_ge(ba_split, 1)
            tt(w_lo[:, 3, 0:512], w_ba_sb, w_hi[:, 3, 0:512].bitcast(F32), ALU.subtract).then_inc(ba_split, 1)
            turn(0)
            for k in range(AHEAD):
                split(0, k)
            flat = lambda k: sc[:, k].rearrange("p t h -> p (t h)")
            ba3 = ba[:, 0:64].rearrange("p (t b h) -> p t b h", t=NT, b=2)
            tb, a2, l, ea, mx = (ba[:, o:o + 32] for o in (64, 96, 160, 192, 224))
            dve.wait_ge(ba_done, 1)
            V.tensor_copy(ba[:, 0:64], J[:, 0, 0:64]).then_inc(ba_link, 1)
            dve.wait_ge(ba_link, 1)
            tt(a2.rearrange("p (t h) -> p t h", t=NT), ba3[:, :, 1], dt_bias.rearrange("p (t h) -> p t h", t=NT),
               ALU.add).then_inc(ba_link, 1)
            dve.wait_ge(ba_link, 2)
            ts(mx, a2, 0.0, None, ALU.max).then_inc(ba_link, 1)
            dve.wait_ge(ba_act, 4)
            dve.wait_ge(ba_link, 3)
            tt(mx, mx, l, ALU.add).then_inc(ba_link, 1)
            dve.wait_ge(ba_link, 4)
            stt(out=flat(G), in0=mx, scalar=-1.0, in1=ea, op0=ALU.mult, op1=ALU.mult).then_inc(g_ready, 1)
            ts(flat(BETA), tb, 0.5, 0.5, ALU.mult, ALU.add)
            ts(flat(BHALF), tb, 0.25, 0.25, ALU.mult, ALU.add).then_inc(ba_link, 1)
            dve.wait_ge(g_ready, 1)
            for ck in range(2):
                ts(flat(CHDEC0 + ck), flat(G), chunk_sel[:, ck:ck + 1], None, ALU.mult).then_inc(g_ready, 1)

            def decay_step(h):
                if h == 10:
                    dve.wait_ge(ba_act, 5)
                    dve.wait_ge(ba_link, 5)
                    tt(flat(K_DEC), J[:, 1, 32:64], flat(DCOL), ALU.subtract).then_inc(ba_link, 1)
                    stt(out=flat(K_OUT), in0=flat(K_OUT), scalar=-1.0, in1=flat(BETA), op0=ALU.mult, op1=ALU.mult
                        ).then_inc(sc_ready, 1)

            def read(q_end, ops):
                def f():
                    dve.wait_ge(chunk_used, RING * q_end)
                    ops()
                return f

            def window(q0, jobs):
                for n in range(4):
                    def ops(n=n):
                        V.tensor_copy(rawg[:, n, 1], acc[:, n % 2, 1]).then_inc(rawg_d, 1)
                    output(q0 + n * (CPO // RING), jobs, read(q0 + (n + 1) * (CPO // RING), ops), h0=16 * n)

            window(0, decay_step)
            with dve.Fori(1, NG) as w:
                window(w * CPO, lambda h: gdn_step(h, w - 1))

            for n in range(5):
                def ops(n=n):
                    if n == 0:
                        dve.wait_ge(front_T, 4 * NG - 3)
                        V.tensor_copy(kdup[:, 1].rearrange("p (k d c) -> p k d c", k=4, d=2),
                                      acc[:, 0, 1, 0:T].rearrange("p (k c) -> p k c", k=4).unsqueeze(2).broadcast_to([P, 4, 2, C]))
                        V.tensor_copy(vs[:, 1], acc[:, 0, 1, T:2 * T]).then_inc(kv_d, 1)
                    else:
                        ts(xres[:, 1, (n - 1) * NB:n * NB], acc[:, n % 2, 1], 0.125, None, ALU.mult).then_inc(sq_d, 1)
                q = (OUT_SWA + n) * (CPO // RING)
                output(q, lambda h: gdn_step(h, NG - 1), read(q + CPO // RING, ops), h0=16 * n)

            with dve.Fori(0, 4) as j:
                q = j * 4 + OUT_MIX1 * 2

                def merge():
                    dve.wait_ge(gate_done, j + 1)
                    dve.wait_ge(qfix_done, j + 1)
                    for t in range(NT):
                        ins = stt(out=xres[:, t, bass.ds(j * NB, NB)], in0=gb[:, t], scalar=1.0, in1=acc[:, 0, t],
                                  op0=ALU.add, op1=ALU.mult)
                    ins.then_inc(merged, 1)
                output(q, lambda h: swa_step(h, j), lambda: None, h0=0)
                output(q + 2, lambda h: swa_step(h, j), read(q + 4, merge), h0=16)
            with dve.Fori(0, 4) as j:
                q = j * 4 + OUT_MIX2 * 2

                def merge():
                    dve.wait_ge(gate_done, j + 5)
                    for t in range(NT):
                        ins = stt(out=gb[:, t], in0=gb[:, t], scalar=1.0, in1=acc[:, 0, t], op0=ALU.add, op1=ALU.mult)
                    ins.then_inc(merge_link, 1)
                    dve.wait_ge(merge_link, j + 1)
                    dst = xres[:, :, bass.ds(j * NB, NB)]
                    tt(dst, dst, gb[:], ALU.add).then_inc(merged, 1)
                output(q, None, lambda: None)
                output(q + 2, None, read(q + 4, merge))
            turn(1)

            def add_x(col):
                def make(par):
                    def ops():
                        for t in range(NT):
                            dst = xres[:, t, col]
                            ins = tt(dst, dst, acc[:, par, t], ALU.add)
                        ins.then_inc(x_added, 1)
                    return ops
                return make

            dve.wait_ge(x_in, 32)
            for i in range(4):
                q = (OUT_WO + i) * 2
                output(q, None, read(q + 2, add_x(slice(i * NB, (i + 1) * NB))(1 - i % 2)))
            dve.wait_ge(r_x, 2)
            dve.wait_ge(x_added, 4)
            ts(nat[:, 1], xres[:, 1], stat[:, 3:4], None, ALU.mult).then_inc(nat_d, 1)
            turn(2)

            def square(p, k):
                def ops():
                    dve.wait_ge(relu_done, k)
                    for t in range(NT):
                        ins = tt(rbuf[:, p, t], acc[:, 1 - p, t], rbuf[:, p, t], ALU.mult)
                    ins.then_inc(relu_sq, 1)
                return ops

            def up_job(b0, kt, cnt):
                def job(h):
                    if h == 2:
                        dve.wait_ge(act_hi_done, cnt)
                        for b in range(2):
                            ins = tt(act_lo[:, bass.ds(kt + 2 * b, 2), :], J[:, b0 + b].rearrange("p (a t) -> p a t", a=2),
                                     act_hi[:, bass.ds(kt + 2 * b, 2), :].bitcast(F32), ALU.subtract)
                        ins.then_inc(act_lo_done, 1)
                return job

            for hf in range(2):
                q0, r0 = (CH_FF + hf * CH_HALF) // RING, FF_UP * hf
                for p in range(2):
                    output(q0 + 2 * p, up_job(0, 0, r0 + 1) if p else None, read(q0 + 2 * p + 2, square(p, r0 + p + 1)))
                with dve.Fori(1, FF_UP // 2) as i:
                    for p in range(2):
                        q = i * 4 + (q0 + 2 * p)
                        output(q, up_job(2 * (1 - p), i * 8 + 4 * (p - 1), i * 2 + (r0 + p)),
                               read(q + 2, square(p, i * 2 + (r0 + p + 1))))
                qd = q0 + FF_UP * 2
                for n in range(FF_DOWN):
                    output(qd + 4 * n, up_job(2, 28, r0 + FF_UP) if n == 0 else None,
                           read(qd + 4 * n + 4, add_x(slice(n * NB, (n + 1) * NB))(1 - n % 2)), nch=2 * CPO)
            dve.wait_ge(r_x, 3)
            dve.wait_ge(dist_in, 32)
            for t in range(NT):
                stt(out=nat[:, t], in0=xres[:, t], scalar=stat[:, 2 + t:3 + t], in1=fgain[:], op0=ALU.mult,
                    op1=ALU.mult).then_inc(y_ready, 1)

        @block.gpsimd
        def _(pool):
            tt, ts = nc.gpsimd.tensor_tensor, nc.gpsimd.tensor_scalar
            nc.gpsimd.memset(stat[:, 4:16], -0.5).then_inc(pool_x, 1)

            def row_factor(k):
                pool.wait_ge(ssq_x, k)
                ts(stat[:, 2:4], stat[:, 0:2], 1.0 / D, EPS, ALU.mult, ALU.add).then_inc(pool_x, 1)
                pool.wait_ge(pool_x, k + 1)
                tt(stat[:, 2:4], stat[:, 2:4], stat[:, 4:6], ALU.pow).then_inc(r_x, 1)

            row_factor(1)

            def group(g):
                def power(i, wait, value, done):
                    pool.wait_ge(wait, value)
                    tt(rg[:, i], rg[:, i], stat[:, 8:16], ALU.pow).then_inc(done, 1)

                pool.wait_ge(par_ready, g + 1)
                tt(mat(M_B0), wide(scu(G), C), over(tri64, U), ALU.mult).then_inc(rows_rhs, 1)
                tt(mat(M_B1), wide(scu(BETA), C), over(eye64, U), ALU.mult).then_inc(rows_rhs, 1)
                power(0, nssq_done, 2 * g + 1, nr_done)
                power(1, nssq_done, 2 * g + 2, nr_done)
                pool.wait_ge(exp_done, g + 1)
                tt(mat(M_KQ), mat(M_X), over(upi, U), ALU.mult).then_inc(mask_done, 1)
                tt(mat(M_B1), mat(M_X), mat(M_B0), ALU.mult).then_inc(mask_done, 1)
                pool.wait_ge(mask_done, 5 * g + 2)
                tt(mat(M_B1), mat(M_B1), over(up, U), ALU.mult).then_inc(mask_done, 1)
                tt(mat(M_V), mat(M_U), over(low, U), ALU.mult).then_inc(mask_done, 1)
                pool.wait_ge(mask_done, 5 * g + 4)
                tt(mat(M_V), mat(M_V), wide(scu(BETA), C), ALU.mult).then_inc(mask_done, 1)
                pool.wait_ge(at_ready, g + 1)
                tt(mat(M_X), mat(M_V), over(nlow1, U), ALU.mult).then_inc(xu_link, 1)
                tt(mat(M_B0), mat(M_AT), over(up_level[0], U), ALU.mult).then_inc(bt_ready, 1)
                pool.wait_ge(xu_link, g + 1)
                tt(mat(M_X), mat(M_X), over(eye64, U), ALU.add).then_inc(x0_ready, 1)
                for lv in range(1, LEVELS):
                    if lv >= 2:
                        pool.wait_ge(vpass, LEVELS * g + (lv - 1))
                    tt(mat(M_B0 + lv % 2), mat(M_AT), over(up_level[lv], U), ALU.mult).then_inc(bt_ready, 1)
                    if lv == 1:
                        pool.wait_ge(qk_T, 2 * g + 1)
                        tt(kn3, kn3, wide(scu(K_DEC), P), ALU.mult).then_inc(kdec_done, 1)
                power(2, ossq_done, g + 1, or_done)

            with pool.Fori(0, NG) as g:
                group(g)
            row_factor(2)
            row_factor(3)


def program(nc, ap, outs):
    hybrid_trunk(nc, ap["x"].rearrange("(t p) d -> p t d", p=P), ap["weights"], ap["w_ba"], ap["colp"], ap["rowp"],
                 ap["masks"], ap["dist"], ap["fgain"], outs.rearrange("(t p) d -> t p d", p=P))


def mask_constants():
    p = np.arange(P)
    same = (p[:, None] // C) == (p[None, :] // C)
    tri = same & (p[:, None] <= p[None, :])
    r, j = (p % C)[:, None], np.arange(C)[None, :]
    small = [r <= j, r == j, r > j, r <= j, r < j]
    nlow1 = -((r // 2 == j // 2) & (r > j)).astype(np.float32)
    nup1 = -((r // 2 == j // 2) & (r < j)).astype(np.float32)
    levels = []
    for lv in range(LEVELS):
        s = 2 << lv
        levels.append((r // (2 * s) == j // (2 * s)) & ((j // s) % 2 == 1) & ((r // s) % 2 == 0))
    parts = [np.eye(P), tri, tri[:, p ^ C], same, np.ones((P, P)), *small, nlow1, nup1, *levels]
    return np.concatenate([np.asarray(a, np.float32) for a in parts], axis=1)


def distances():
    q, k = np.arange(P)[:, None], np.arange(P)[None, :]
    own = np.where(q >= k, k - q, NEG)
    prev = np.where(k > q, k - q - P, NEG)
    return np.concatenate([own, prev, own], axis=1).astype(np.float32)


def kernel(**inputs):
    import numpy as _np
    import concourse.bacc as _bacc
    from concourse import mybir as _mybir
    from concourse.bass_utils import run_bass_kernel_spmd as _run

    a = {k: _np.asarray(v) for k, v in inputs.items()}
    w_in = a["w_in"][0]
    W = 4 * D
    b0, sq0, sk0, sv0, gt0 = W, W + 32, W + 32 + D, W + 32 + D + 256, W + 32 + D + 512

    def chunks(w):
        return w.reshape(-1, CK, P, NB).transpose(0, 2, 1, 3).reshape(-1, P, CK * NB)

    stream = []
    for g in range(NG):
        for base in (D, 0, 2 * D, 3 * D):
            stream.append(chunks(w_in[:, base + g * NB:base + (g + 1) * NB]))
    stream.append(chunks(w_in[:, sk0:sk0 + NB]))
    for i in range(4):
        stream.append(chunks(w_in[:, sq0 + i * NB:sq0 + (i + 1) * NB]))
    for base, w in ((gt0, a["w_branch_gdn"][0]), (gt0 + D, a["w_branch_swa"][0])):
        for i in range(4):
            stream.append(chunks(w_in[:, base + i * NB:base + (i + 1) * NB]))
            stream.append(chunks(w[:, i * NB:(i + 1) * NB]))
    for i in range(4):
        stream.append(chunks(a["w_out"][0][:, i * NB:(i + 1) * NB]))
    for hf in range(2):
        for i in range(FF_UP):
            o = hf * (DFF // 2) + i * NB
            stream.append(chunks(a["w_ff_up"][0][:, o:o + NB]))
        for i in range(FF_DOWN):
            stream.append(chunks(a["w_ff_down"][0][hf * (DFF // 2):(hf + 1) * (DFF // 2), i * NB:(i + 1) * NB]))

    def column(v):
        return v.reshape(-1, P).T

    conv = a["conv_w"][0].reshape(4, 3, KT, P)[:, [1, 0, 2]].transpose(3, 1, 2, 0).reshape(P, 192)
    sel = _np.repeat(_np.eye(2, dtype=_np.float32), C, axis=0)
    slopes = (2.0 ** (-8.0 * _np.arange(1, 33) / 32)).astype(_np.float32)
    rows = [_np.tile(a["dt_bias"][0], 2), _np.tile(a["a_log"][0], 2), slopes, a["attn_sinks"][0]]
    arrays = {
        "x": a["x"][0],
        "weights": _np.concatenate(stream),
        "w_ba": w_in[:, b0:b0 + 32].reshape(KT, P, 32).transpose(1, 0, 2).reshape(P, 512),
        "colp": _np.concatenate([conv, column(a["norm1_g"][0]), column(a["norm2_g"][0]), column(a["gdn_norm_g"][0]), sel],
                                axis=1),
        "rowp": _np.tile(_np.concatenate(rows)[None, :], (P, 1)),
        "masks": mask_constants(),
        "dist": distances(),
        "fgain": _np.tile(a["final_norm_g"][None, :], (P, 1)),
    }
    nc = _bacc.Bacc("TRN2", target_bir_lowering=False, num_devices=1)
    arrays = {k: _np.ascontiguousarray(v) for k, v in arrays.items()}
    ap = {k: nc.dram_tensor(k, v.shape, _mybir.dt.from_np(v.dtype), kind="ExternalInput").ap() for k, v in arrays.items()}
    y = nc.dram_tensor("y", (T, D), F32, kind="ExternalOutput").ap()
    program(nc, ap, y)
    r = _run(nc, [arrays], core_ids=[0])
    return r.results[0]["y"].reshape(1, T, D)
```

```python
from contextlib import ExitStack

import concourse.bass as bass
from concourse import mybir
import numpy as np

ALU = mybir.AluOpType
ACT = mybir.ActivationFunctionType
F32 = mybir.dt.float32
F32R = mybir.dt.float32r
AX_X = mybir.AxisListType.X

P = 128
T = 256
NT = T // P
D = 2048
KT = D // P
DFF = 4 * D
NB = 512
HG = 4
NG = 4
C = 64
NCH = T // C
U = NT * HG
HQ = 8
CK = 2
CPO = KT // CK
RING = 4
AHEAD = 3
EPS = 1e-6
NEG = -3.0e38
LEVELS = 5

OUT_SWA = 4 * NG
OUT_MIX1 = OUT_SWA + 5
OUT_MIX2 = OUT_MIX1 + 8
OUT_WO = OUT_MIX2 + 8
OUT_FF = OUT_WO + 4
FF_UP, FF_DOWN = 8, 4
CH_FF = OUT_FF * CPO
CH_HALF = FF_UP * CPO + FF_DOWN * 2 * CPO
N_CHUNKS = CH_FF + 2 * CH_HALF

G, BETA, BHALF, K_OUT, Q_OUT, K_DEC, DCOL, CHDEC0, CHDEC1 = range(9)
M_AT, M_X, M_U, M_V, M_B0, M_B1, M_KQ = range(7)
ITEM_K, ITEM_Q, ITEM_V, ITEM_Z = range(4)
FRONT = {ITEM_K: 0, ITEM_Q: 1, ITEM_V: 25, ITEM_Z: 37}
BANK = {ITEM_K: 0, ITEM_Q: 2, ITEM_V: 2, ITEM_Z: 2}
TAPS = {ITEM_K: (0, 1, 2), ITEM_Q: (3, 5, 7), ITEM_V: (26, 28, 31)}
TANH = {ITEM_K: 3, ITEM_Q: 9, ITEM_V: 32}
SILU = {ITEM_K: 4, ITEM_Q: 10, ITEM_V: 33}
BACK = {ITEM_K: 10, ITEM_Q: 16, ITEM_V: 34}
NORM = {ITEM_K: 13, ITEM_Q: 19}
ROWS, TK, TQ, KKQ, INV, QTM, OT = 11, 16, 21, 22, 25, 40, 63
P1, P2, P3 = (40, 45, 50, 55), (42, 47, 52, 57), (44, 49, 54, None)
SCORE = tuple(4 + 8 * s // 3 for s in range(8))
PTURN = tuple(h + 5 for h in SCORE)
PV = tuple(SCORE[s | 1] + 8 - (s + 1) % 2 for s in range(8))


def hybrid_trunk(nc, x, weights, w_ba, colp_d, rowp_d, masks_d, dist_d, fgain_d, out):
    with ExitStack() as ctx:
        def sb(name, shape, dt=F32, where=ctx):
            return where.enter_context(nc.sbuf_tensor(name, shape, dt))

        def sem(name):
            return ctx.enter_context(nc.semaphore(name))

        raw = sb("raw", [P, RING, CK * NB])
        w_hi = sb("w_hi", [P, RING, CK * NB], F32R)
        w_lo = sb("w_lo", [P, RING, CK * NB], F32R)
        hT_hi = sb("hT_hi", [P, KT, T], F32R)
        hT_lo = sb("hT_lo", [P, KT, T], F32R)
        xres = sb("xres", [P, NT, D])
        masks = sb("masks_sb", [P, 5 * P + 12 * C])
        colp = sb("colp_sb", [P, 48 * 4 + 2 * KT + 3])
        rowp = sb("rowp_sb", [P, 128])
        stat = sb("stat", [P, 16])
        part = sb("part", [P, NT, 4])
        kT = sb("kT", [P, 4, T])
        vs = sb("vs", [P, NT, 4 * C])

        with ExitStack() as first:
            wba_hi = sb("wba_hi", [P, NB], F32R, first)
            wba_lo = sb("wba_lo", [P, NB], F32R, first)
        with ExitStack() as mixers:
            og_hi = sb("og_hi", [P, KT, T], F32R, mixers)
            og_lo = sb("og_lo", [P, KT, T], F32R, mixers)
            with ExitStack() as gdn:
                rawg = sb("rawg", [P, 4, NT, NB], where=gdn)
                cT = sb("cT", [P, HG, T], where=gdn)
                vb = sb("vb", [P, NT, NB], where=gdn)
                kn = sb("kn", [P, NT, NB], where=gdn)
                qn = sb("qn", [P, NT, NB], where=gdn)
                kq = sb("kq", [P, HG, NCH * P], where=gdn)
                zs = sb("zs", [P, HG, T], where=gdn)
                mats = sb("mats", [P, 7, U, C], where=gdn)
                solve = sb("solve", [P, U, 2, C], where=gdn)
                S = sb("S", [P, HG, P], where=gdn)
                sc = sb("sc", [P, 9, NT, 16], where=gdn)
                scg = sb("scg", [P, 9, NT, HG], where=gdn)
                cwg = sb("cwg", [P, 3, HG, 4], where=gdn)
                rg = sb("rg", [P, 3, 8], where=gdn)
            with ExitStack() as swa:
                os_hi = sb("os_hi", [P, KT, T], F32R, swa)
                os_lo = sb("os_lo", [P, KT, T], F32R, swa)
                gb = sb("gb", [P, NT, NB], where=swa)
                qfix = sb("qfix", [P, NT, NB], where=swa)
                qTs = sb("qTs", [P, 4, T], where=swa)
                kfix = sb("kfix", [P, T], where=swa)
                vfix = sb("vfix", [P, NT, C], where=swa)
                dist = sb("dist_sb", [P, 3 * P], where=swa)
                sbuf_s = sb("sbuf_s", [P, 2, 3 * P], where=swa)
                prob = sb("prob", [P, 2, 3 * P], where=swa)
                probT = sb("probT", [P, 2, 3 * P], where=swa)
                oS = sb("oS", [P, NT, NB], where=swa)
                slf = sb("slf", [P, 2, HQ], where=swa)
                r3 = sb("r3", [P, HQ, 3], where=swa)
                negm = sb("negm", [P, HQ, 2], where=swa)
                lsum = sb("lsum", [P, HQ, 2], where=swa)
                esink = sb("esink", [P, HQ, 2], where=swa)
        with ExitStack() as mlp:
            act_hi = sb("act_hi", [P, 32, T], F32R, mlp)
            act_lo = sb("act_lo", [P, 32, T], F32R, mlp)
            rbuf = sb("rbuf", [P, 2, NT, NB], where=mlp)
            nat = sb("nat", [P, NT, D], where=mlp)
            fgain = sb("fgain_sb", [P, D], where=mlp)

        acc = ctx.enter_context(nc.psum_tensor("acc", [P, 2, NT, NB], F32))
        J = ctx.enter_context(nc.psum_tensor("J", [P, 4, NB], F32))

        ident, tri, tri_swap, chunk_ones, ones = (masks[:, i * P:(i + 1) * P] for i in range(5))
        (tri64, eye64, low, upi, up, nlow1, nup1, *up_level) = (
            masks[:, 5 * P + i * C:5 * P + (i + 1) * C] for i in range(12))
        conv_w = colp[:, 0:192].rearrange("p (k n c) -> p k n c", k=3, c=4)
        gain_cols = (colp[:, 192:192 + KT], None, colp[:, 192 + KT:192 + 2 * KT])
        gdn_gain = colp[:, 224:225]
        chunk_sel = colp[:, 225:227]
        dt_bias, a_log = rowp[:, 0:32], rowp[:, 32:64]
        slopes, sinks = rowp[:, 64:96], rowp[:, 96:128]
        RH = mats[:, M_B0].rearrange("p u c -> p (u c)")
        VO = mats[:, M_V].rearrange("p u c -> p (u c)")
        qnT, vbT = (a[:].rearrange("p t n -> p (t n)").rearrange("p (h t) -> p h t", h=HG) for a in (qn, vb))
        qn3, kn3, vb3 = (a[:].rearrange("p t (h e) -> p (t h) e", h=HG) for a in (qn, kn, vb))
        cT2 = cT[:].rearrange("p h t -> p (h t)")
        cTu = cT[:].rearrange("p h (t e) -> p (h t) e", t=NT)
        nat1 = rawg[:].rearrange("p a t n -> p (a t n)").rearrange("p (t d) -> p t d", t=NT)
        w_ba_sb = zs[:].rearrange("p h t -> p (h t)")[:, 0:512]
        ba = vb[:].rearrange("p t n -> p (t n)")
        kdup = rawg[:, 0]

        def mat(i):
            return mats[:, i]

        def scu(kind):
            return scg[:, kind].rearrange("p t h -> p (t h)")

        def wide(a, n):
            return a.unsqueeze(2).broadcast_to([a.shape[0], a.shape[1], n])

        def over(a, n):
            return a.unsqueeze(1).broadcast_to([a.shape[0], n, a.shape[1]])

        step_begun = sem("step_begun")
        params_in, x_in, x_back, raw_in = sem("params_in"), [sem(f"x_in{i}") for i in range(4)], [sem(f"x_back{i}") for i in range(4)], [sem(f"raw_in{i}") for i in range(RING)]
        hi_ready, lo_ready, chunk_used = sem("hi_ready"), sem("lo_ready"), sem("chunk_used")
        ssq_x, sum_link, sum_ready, half_ready, r_x, nat_a, nat_d = (
            sem(n) for n in ("ssq_x", "sum_link", "sum_ready", "half_ready", "r_x", "nat_a", "nat_d"))
        turn_T, turn_hi, turn_lo = sem("turn_T"), sem("turn_hi"), sem("turn_lo")
        wba_ready, ba_done, ba_link, ba_act = (sem(n) for n in ("wba_ready", "ba_done", "ba_link", "ba_act"))
        g_ready, decay_done, sc_ready = sem("g_ready"), sem("decay_done"), sem("sc_ready")
        rawg_a, rawg_d, par_ready = sem("rawg_a"), sem("rawg_d"), sem("par_ready")
        front_T, conv_0, conv_tap, tanh_done, silu_done, back_T = (
            sem(n) for n in ("front_T", "conv_0", "conv_tap", "tanh_done", "silu_done", "back_T"))
        vb_done, nsq_done, nssq_done, nr_link, nr_done, norm_done = (
            sem(n) for n in ("vb_done", "nsq_done", "nssq_done", "nr_link", "nr_done", "norm_done"))
        qk_T, kq_a, kq_d = sem("qk_T"), sem("kq_a"), sem("kq_d")
        rows_rhs, rows_done, arg_done, exp_done, mask_done = (
            sem(n) for n in ("rows_rhs", "rows_done", "arg_done", "exp_done", "mask_done"))
        kkq_done, at_ready, x0_link, xu_link, x0_ready, u0_ready, bt_ready, vpass, vcopy, zpass, inv_done = (
            sem(n) for n in ("kkq_done", "at_ready", "x0_link", "xu_link", "x0_ready", "u0_ready", "bt_ready", "vpass", "vcopy", "zpass", "inv_done"))
        qt_done, qt_copied, kdec_done = sem("qt_done"), sem("qt_copied"), sem("kdec_done")
        s_ready, p1_done, rh_done, p2_done, vo_done, o_done, p3_done = (
            sem(n) for n in ("s_ready", "p1_done", "rh_done", "p2_done", "vo_done", "o_done", "p3_done"))
        osq_done, ossq_done, or_done, on_done, o_T, og_f, og_hi_done, og_lo_done = (
            sem(n) for n in ("osq_done", "ossq_done", "or_done", "on_done", "o_T", "og_f", "og_hi_done", "og_lo_done"))
        kv_a, kv_d, kv_T, kT_done, sq_a, sq_d = (sem(n) for n in ("kv_a", "kv_d", "kv_T", "kT_done", "sq_a", "sq_d"))
        dist_in, qfix_done, fix_done, q_T, qT_a, qT_d = (
            sem(n) for n in ("dist_in", "qfix_done", "fix_done", "q_T", "qT_a", "qT_d"))
        score_done, bias_done, max_link, negm_done, exps_done = (
            sem(n) for n in ("score_done", "bias_done", "max_link", "negm_done", "exps_done"))
        p_T, pT_copied, pv_done, l_link, oS_done = (sem(n) for n in ("p_T", "pT_copied", "pv_done", "l_link", "oS_done"))
        oS_T, os_hi_done, os_lo_done = sem("oS_T"), sem("os_hi_done"), sem("os_lo_done")
        gate_done, merged, merge_link = sem("gate_done"), sem("merged"), sem("merge_link")
        relu_done, relu_sq, up_T, act_hi_done, act_lo_done = (
            sem(n) for n in ("relu_done", "relu_sq", "up_T", "act_hi_done", "act_lo_done"))
        x_added, y_ready, y_out = sem("x_added"), sem("y_ready"), sem("y_out")

        block = ctx.enter_context(nc.Block())

        @block.sync
        def _(sp):
            for i in range(4):
                sp.dma_start(xres[:, :, i * NB:(i + 1) * NB], x[:, :, i * NB:(i + 1) * NB]).then_inc(x_in[i], 16)
            for dst, src in ((masks, masks_d), (colp, colp_d), (rowp, rowp_d)):
                sp.dma_start(dst[:], src).then_inc(params_in, 16)
            sp.dma_start(w_ba_sb, w_ba).then_inc(params_in, 16)
            for i in range(RING):
                sp.dma_start(raw[:, i], weights[i]).then_inc(raw_in[i], 16)

            def stream(a, b):
                with sp.Fori(a, b) as q:
                    for i in range(RING):
                        sp.wait_ge(lo_ready, RING * q + (i - RING + 1))
                        sp.dma_start(raw[:, i], weights[bass.ds(RING * q + i, 1)].rearrange(
                            "a p n -> p (a n)")).then_inc(raw_in[i], 16)

            first_swa = OUT_MIX1 * CPO // RING
            stream(1, first_swa)
            sp.wait_ge(og_lo_done, 2 * NG)
            sp.dma_start(dist[:], dist_d).then_inc(dist_in, 16)
            stream(first_swa, OUT_FF * CPO // RING)
            sp.dma_start(fgain[:], fgain_d).then_inc(dist_in, 16)
            stream(OUT_FF * CPO // RING, N_CHUNKS // RING)
            for i in range(4):
                sp.wait_ge(y_ready, i + 1)
                sp.dma_start(out[:, :, i * NB:(i + 1) * NB], nat[:, :, i * NB:(i + 1) * NB]).then_inc(y_out, 16)
            sp.wait_ge(y_out, 16 * 4)

        @block.tensor
        def _(pe):
            mm, tr = nc.tensor.matmul, nc.tensor.transpose

            def output(c0, par, aT_hi, aT_lo, free, jobs=None, nch=CPO, h0=0, before=None):
                for c in range(nch):
                    if before:
                        before(c)
                    pe.wait_ge(lo_ready, c0 + (c + 1))
                    if c == 0:
                        for s_free, v in free:
                            if not isinstance(v, int) or v > 0:
                                pe.wait_ge(s_free, v)
                    for k in range(CK):
                        kt = c * CK + k
                        w = slice(k * NB, (k + 1) * NB)
                        for t in range(NT):
                            tok = slice(t * P, (t + 1) * P)
                            o = acc[:, par, t]
                            mm(o, aT_hi[:, kt, tok], w_hi[:, c % RING, w], start=(c == 0 and k == 0), stop=False)
                            mm(o, aT_hi[:, kt, tok], w_lo[:, c % RING, w], start=False, stop=False)
                            last = mm(o, aT_lo[:, kt, tok], w_hi[:, c % RING, w], start=False,
                                      stop=(c == nch - 1 and k == CK - 1))
                        if k == CK - 1:
                            last.then_inc(chunk_used, 1)
                        if jobs:
                            jobs(h0 + c * CK + k)

            def turning(k, src, ready):
                def bank(i):
                    ready(i // 2)
                    if 8 * k + i >= 4:
                        pe.wait_ge(turn_lo, 8 * k + i - 3)
                    for kk in range(2):
                        for t in range(NT):
                            kt = 2 * i + kk
                            ins = tr(J[:, i % 4, kk * T + t * P:kk * T + (t + 1) * P],
                                     src[:, t, kt * P:(kt + 1) * P], ident)
                    ins.then_inc(turn_T, 1)

                def before(c):
                    for i in ((0, 1, 2) if c == 0 else (c + 2,)):
                        if i < CPO:
                            bank(i)
                    pe.wait_ge(turn_lo, 8 * k + c + 1)
                return before

            def turn_group(src, b0, sem_, dst_cols=None):
                for m in range(HG):
                    for t in range(NT):
                        ins = tr(J[:, b0 + m // 2, (m % 2) * T + t * P:(m % 2) * T + (t + 1) * P],
                                 src[:, t, m * P:(m + 1) * P], ident)
                ins.then_inc(sem_, 1)

            def gdn_step(h, g):
                for n in range(4):
                    if h == FRONT[n]:
                        pe.wait_ge(rawg_a, 4 * g + (n + 1))
                        if n == ITEM_K:
                            pe.wait_ge(og_f, 2 * g + 2)
                        if n == ITEM_V:
                            pe.wait_ge(at_ready, g + 1)
                        if n == ITEM_Z:
                            pe.wait_ge(vb_done, g + 1)
                        turn_group(rawg[:, n], BANK[n], front_T)
                for n in (ITEM_K, ITEM_Q, ITEM_V):
                    if h == BACK[n]:
                        pe.wait_ge(silu_done, 4 * g + (n + 1))
                        if n == ITEM_Q:
                            pe.wait_ge(exp_done, g + 1)
                        src = qnT if n == ITEM_Q else cT
                        for t in range(NT):
                            for m in range(HG):
                                ins = tr(J[:, BANK[n] + t, m * P:(m + 1) * P], src[:, m, t * P:(t + 1) * P], ident)
                        ins.then_inc(back_T, 1)
                if h == TK or h == TQ:
                    n = 0 if h == TK else 1
                    pe.wait_ge(norm_done, 2 * g + (n + 1))
                    src = qn if n else kn
                    for t in range(NT):
                        for m in range(HG):
                            ins = tr(J[:, 2 * n + t, m * P:(m + 1) * P], src[:, t, m * P:(m + 1) * P], ident)
                    ins.then_inc(qk_T, 1)
                if h == ROWS:
                    pe.wait_ge(rows_rhs, 2 * g + 2)
                    pe.wait_ge(conv_tap, 9 * g + 6)
                    mm(J[:, 2], chunk_ones, mat(M_B0), start=True, stop=True)
                    mm(J[:, 3], chunk_ones, mat(M_B1), start=True, stop=True).then_inc(rows_done, 1)
                if h == KKQ:
                    pe.wait_ge(kq_a, 2 * g + 2)
                    pe.wait_ge(kq_d, g + 1)
                    pe.sem_inc(step_begun, 1)
                    for bank in range(2):
                        for u in range(U):
                            t, hd = divmod(u, HG)
                            for ck in range(2):
                                c = 2 * t + ck
                                kc = kq[:, hd, c * P + ck * C:c * P + ck * C + C]
                                qc = kq[:, hd, c * P + (1 - ck) * C:c * P + (1 - ck) * C + C]
                                ins = mm(J[ck * C:ck * C + C, 2 + bank, u * C:(u + 1) * C], kc,
                                         qc if bank else kc, start=True, stop=True)
                    ins.then_inc(kkq_done, 1)

                def per_chunk(bank, lhs, rhs, done):
                    for u in range(U):
                        for ck in range(2):
                            r = slice(ck * C, ck * C + C)
                            ins = mm(J[r, bank, u * C:(u + 1) * C], lhs[r, u], rhs[r, u], start=True, stop=True)
                    if done is not None:
                        ins.then_inc(done, 1)

                for lv in range(LEVELS):
                    if h == INV + 3 * lv:
                        pe.wait_ge(bt_ready, LEVELS * g + (lv + 1))
                        if lv:
                            pe.wait_ge(inv_done, LEVELS * g + lv)
                        else:
                            pe.wait_ge(x0_ready, g + 1)
                        pe.sem_inc(step_begun, 1)
                        per_chunk(0, mat(M_B0 + lv % 2), mat(M_X), vpass)
                    if h == INV + 3 * lv + 1:
                        pe.wait_ge(vcopy, LEVELS * g + (lv + 1))
                        if lv == 0:
                            pe.wait_ge(u0_ready, 2 * g + 2)
                        pe.sem_inc(step_begun, 1)
                        per_chunk(1, mat(M_U), mat(M_V), None)
                        per_chunk(0, mat(M_V), mat(M_U), zpass)
                if h == QTM:
                    pe.wait_ge(inv_done, LEVELS * (g + 1))
                    pe.wait_ge(silu_done, 4 * g + 4)
                    pe.sem_inc(step_begun, 1)
                    per_chunk(3, mat(M_X), mat(M_KQ), qt_done)
                for c in range(NCH):
                    t, ck = divmod(c, 2)
                    kr = slice(ck * C, ck * C + C)
                    if h == P1[c]:
                        pe.wait_ge(s_ready, NCH * g + (c + 1))
                        if c:
                            pe.wait_ge(o_done, NCH * g + c)
                        for hd in range(HG):
                            ins = mm(J[:, 0, hd * P:(hd + 1) * P], kq[:, hd, c * P:(c + 1) * P], S[:, hd],
                                     start=True, stop=True)
                        ins.then_inc(p1_done, 1)
                    if h == P2[c]:
                        pe.wait_ge(rh_done, NCH * g + (c + 1))
                        if c == 0:
                            pe.wait_ge(qt_copied, g + 1)
                        for hd in range(HG):
                            ins = mm(J[:, 1, hd * P:(hd + 1) * P], solve[kr, t * HG + hd].rearrange("p a c -> p (a c)"),
                                     RH[kr, hd * P:(hd + 1) * P], start=True, stop=True)
                        ins.then_inc(p2_done, 1)
                    if h == P3[c]:
                        pe.wait_ge(vo_done, NCH * g + (c + 1))
                        if c == 0:
                            pe.wait_ge(kdec_done, g + 1)
                        for hd in range(HG):
                            ins = mm(J[:, 2, hd * P:(hd + 1) * P], kn[kr, t, hd * P:(hd + 1) * P],
                                     VO[kr, hd * P:(hd + 1) * P], start=True, stop=True)
                        ins.then_inc(p3_done, 1)
                if h == OT:
                    pe.wait_ge(on_done, g + 1)
                    turn_group(qn, 0, o_T)

            def swa_step(h, j):
                if h == 3:
                    pe.wait_ge(qfix_done, j + 1)
                    pe.wait_ge(fix_done, j + 1)
                    turn_group(qfix, 0, q_T)
                for s in range(HQ):
                    r = slice((s % 2) * C, (s % 2) * C + C)
                    pb = s % 2
                    if h == SCORE[s]:
                        if s == 0:
                            pe.wait_ge(qT_a, j + 1)
                            pe.wait_ge(qT_d, j + 1)
                            pe.wait_ge(fix_done, j + 1)
                        if s >= 2:
                            pe.wait_ge(bias_done, HQ * j + (s - 1))
                        mm(J[:, pb, 0:P], qTs[r, s // 2, 0:P], kfix[r, 0:P], start=True, stop=True)
                        mm(J[:, pb, P:3 * P], qTs[r, s // 2, P:T], kfix[r, 0:T], start=True,
                           stop=True).then_inc(score_done, 1)
                    if h == PTURN[s]:
                        pe.wait_ge(exps_done, HQ * j + (s + 1))
                        if s:
                            pe.wait_ge(pT_copied, HQ * j + s)
                        for i in range(3):
                            ins = tr(J[:, 2, i * P:(i + 1) * P], prob[:, pb, i * P:(i + 1) * P], ident)
                        ins.then_inc(p_T, 1)
                    if h == PV[s]:
                        pe.wait_ge(pT_copied, HQ * j + (s + 1))
                        if s and s % 2 == 0:
                            pe.wait_ge(oS_done, HQ // 2 * j + s // 2)
                        o = J[:, 3, (s % 4) * P:(s % 4 + 1) * P]
                        mm(o[:, 0:C], probT[:, pb, 0:P], vfix[:, 0], start=True, stop=True)
                        mm(o[:, C:P], probT[:, pb, P:2 * P], vfix[:, 0], start=True, stop=False)
                        mm(o[:, C:P], probT[:, pb, 2 * P:3 * P], vfix[:, 1], start=False, stop=True).then_inc(pv_done, 1)
                if h == 31:
                    pe.wait_ge(oS_done, HQ // 2 * (j + 1))
                    turn_group(oS, 0, oS_T)

            def decay_step(h):
                if h == 16:
                    pe.wait_ge(wba_ready, 2)
                    for t in range(NT):
                        tok = slice(t * P, (t + 1) * P)
                        for kt in range(KT):
                            w = slice(kt * 32, (kt + 1) * 32)
                            o = J[:, 0, t * 32:(t + 1) * 32]
                            mm(o, hT_hi[:, kt, tok], wba_hi[:, w], start=(kt == 0), stop=False)
                            mm(o, hT_hi[:, kt, tok], wba_lo[:, w], start=False, stop=False)
                            ins = mm(o, hT_lo[:, kt, tok], wba_hi[:, w], start=False, stop=(kt == KT - 1))
                    ins.then_inc(ba_done, 1)
                if h == 32:
                    pe.wait_ge(g_ready, 3)
                    gall = sc[:, G].rearrange("p t h -> p (t h)")
                    for i, lhs in enumerate((tri, chunk_ones, tri_swap)):
                        mm(J[:, 1, i * 32:(i + 1) * 32], lhs, gall, start=True, stop=True)
                    mm(J[:, 1, 96:160], ones, sc[:, CHDEC0:CHDEC1 + 1].rearrange("p c t h -> p (c t h)"),
                       start=True, stop=True).then_inc(decay_done, 1)

            def nat_block(k):
                def ready(i):
                    pe.wait_ge(nat_a, 4 * k + i + 1)
                    pe.wait_ge(nat_d, 4 * k + i + 1)
                return ready

            def window(w, jobs):
                for n in range(4):
                    free = [] if isinstance(w, int) and n < 2 else [(rawg_a, 4 * w + (n - 1)), (rawg_d, 4 * w + (n - 1))]
                    turned = turning(0, nat1, nat_block(0)) if isinstance(w, int) and n == 0 else None
                    output(w * (4 * CPO) + n * CPO, n % 2, hT_hi, hT_lo, free, jobs, h0=16 * n, before=turned)

            pe.wait_ge(params_in, 64)
            window(0, decay_step)
            with pe.Fori(1, NG) as w:
                window(w, lambda h: gdn_step(h, w - 1))

            def kv_step(h):
                gdn_step(h, NG - 1)
                if h == 66:
                    pe.wait_ge(kv_a, 1)
                    pe.wait_ge(kv_d, 1)
                    for m in range(4):
                        for t in range(NT):
                            ins = tr(J[:, 2 + m // 2, (m % 2) * T + t * P:(m % 2) * T + (t + 1) * P],
                                     kdup[:, t, m * P:(m + 1) * P], ident)
                    ins.then_inc(kv_T, 1)

            free5 = [[(rawg_a, 15), (rawg_d, 15)], [(rawg_a, 16), (rawg_d, 16)], [(kv_a, 1), (kv_d, 1)],
                     [(sq_a, 1), (sq_d, 1)], [(sq_a, 2), (sq_d, 2)]]
            for n in range(5):
                output((OUT_SWA + n) * CPO, n % 2, hT_hi, hT_lo, free5[n], kv_step, h0=16 * n)

            pe.wait_ge(og_hi_done, 2 * NG)
            pe.wait_ge(og_lo_done, 2 * NG)
            pe.wait_ge(kT_done, 1)
            pe.wait_ge(sq_a, 3)
            pe.wait_ge(sq_d, 3)
            def mix1(j):
                c0 = j * (2 * CPO) + OUT_MIX1 * CPO
                output(c0, 1, hT_hi, hT_lo, [(gate_done, j)], lambda h: swa_step(h, j), h0=0)
                output(c0 + CPO, 0, og_hi, og_lo, [(sq_a, 4), (sq_d, 4), (merged, j)], lambda h: swa_step(h, j), h0=16)
            mix1(0)
            with pe.Fori(1, 4) as j:
                mix1(j)
            with pe.Fori(0, 4) as j:
                c0 = j * (2 * CPO) + OUT_MIX2 * CPO
                output(c0, 1, hT_hi, hT_lo, [(gate_done, j + 4)])
                output(c0 + CPO, 0, os_hi, os_lo, [(os_lo_done, 4), (merged, j + 4)])

            for i in range(4):
                turned = turning(1, xres, lambda b: pe.wait_ge(merged, 5 + b)) if i == 0 else None
                output((OUT_WO + i) * CPO, 1 - i % 2, og_hi, og_lo, [(x_added, i - 1)] if i >= 2 else [(gate_done, 8)],
                       before=turned)

            def up_out(p, c0, prev, free, before=None):
                def job(h):
                    if prev is not None and h == 2:
                        pe.wait_ge(relu_sq, prev)
                        if not isinstance(prev, int) or prev > 1:
                            pe.wait_ge(act_lo_done, prev - 1)
                        turn_group(rbuf[:, 1 - p], 2 * (1 - p), up_T)
                output(c0, 1 - p, hT_hi, hT_lo, free, job, before=before)

            for hf in range(2):
                c0, r0, x0 = CH_FF + hf * CH_HALF, FF_UP * hf, 4 + 4 * hf
                for p in range(2):
                    up_out(p, c0 + p * CPO, (r0 + p) if p else None, [(x_added, x0 - 1 + p)],
                           turning(2, nat, nat_block(1)) if hf == 0 and p == 0 else None)
                with pe.Fori(1, FF_UP // 2) as i:
                    for p in range(2):
                        up_out(p, i * (2 * CPO) + (c0 + p * CPO), i * 2 + (r0 + p), [(relu_sq, i * 2 + (r0 + p - 1))])
                cd = c0 + FF_UP * CPO

                def last_T(h):
                    if h == 2:
                        pe.wait_ge(relu_sq, r0 + FF_UP)
                        pe.wait_ge(act_lo_done, r0 + FF_UP - 1)
                        turn_group(rbuf[:, 1], 2, up_T)
                    if h == 27:
                        pe.wait_ge(act_lo_done, r0 + FF_UP)

                pe.wait_ge(act_lo_done, r0 + FF_UP - 1)
                for d in range(FF_DOWN):
                    output(cd + d * 2 * CPO, 1 - d % 2, act_hi, act_lo,
                           [(relu_sq, r0 + 7 + d)] if d < 2 else [(x_added, x0 + d - 1)],
                           last_T if d == 0 else None, nch=2 * CPO)

        @block.scalar
        def _(act):
            A = nc.scalar.activation

            def split(q, k):
                slot, dq = k % RING, k // RING
                if isinstance(q, int) and RING * q + k >= N_CHUNKS:
                    return
                act.wait_ge(raw_in[slot], 16 * (q + (dq + 1)))
                if not isinstance(q, int) or RING * q + k > RING - 1:
                    act.wait_ge(chunk_used, RING * q + (k - RING + 1))
                A(w_hi[:, slot], raw[:, slot], ACT.Copy).then_inc(hi_ready, 1)

            def output(q0, jobs, epilogue, nch=CPO, h0=0, turned=None):
                for c in range(nch):
                    split(q0, c + AHEAD)
                    if turned is not None and c + 3 < CPO:
                        turn(turned, c + 3)
                    for k in range(CK):
                        if jobs:
                            jobs(h0 + c * CK + k)
                epilogue()

            def turn(k, i):
                dst = og_hi if k == 1 else hT_hi
                act.wait_ge(turn_T, 8 * k + i + 1)
                if k == 1:
                    A(dst[:, 2 * i:2 * i + 2, :], J[:, i % 4].rearrange("p (a t) -> p a t", a=2), ACT.Copy,
                      scale=0.5).then_inc(turn_hi, 1)
                    return
                for kk in range(2):
                    ins = A(dst[:, 2 * i + kk, :], J[:, i % 4, kk * T:(kk + 1) * T], ACT.Copy,
                            scale=gain_cols[k][:, 2 * i + kk:2 * i + kk + 1])
                ins.then_inc(turn_hi, 1)

            def squares(i, dst):
                w = slice(i * NB, (i + 1) * NB)
                for t in range(NT):
                    ins = A(dst[:, t, w], xres[:, t, w], ACT.Square, accum_out=part[:, t, i:i + 1])
                ins.then_inc(ssq_x, 1)

            def norm_rows(k, dst):
                act.wait_ge(r_x, k + 1)
                for i in range(4):
                    w = slice(i * NB, (i + 1) * NB)
                    A(dst[:, 0, w], xres[:, 0, w], ACT.Copy, scale=stat[:, 2:3]).then_inc(nat_a, 1)

            def gdn_step(h, g):
                if h == FRONT[ITEM_Z]:
                    act.wait_ge(front_T, 4 * g + 4)
                    act.wait_ge(silu_done, 4 * g + 3)
                    for b in range(2):
                        ins = A(zs[:, 2 * b:2 * b + 2].rearrange("p a t -> p (a t)"), J[:, 2 + b], ACT.Tanh, scale=0.5)
                    ins.then_inc(tanh_done, 1)
                for n in (ITEM_K, ITEM_Q, ITEM_V):
                    if h == FRONT[n]:
                        act.wait_ge(front_T, 4 * g + (n + 1))
                        if n == ITEM_K:
                            act.wait_ge(par_ready, g + 1)
                        else:
                            if n == ITEM_V:
                                act.wait_ge(back_T, 3 * g + 2)
                        dst = qnT if n == ITEM_Q else cT
                        for m in range(HG):
                            ins = A(dst[:, m], J[:, BANK[n] + m // 2, (m % 2) * T:(m % 2 + 1) * T], ACT.Copy,
                                    scale=cwg[:, n, m, 3:4])
                        ins.then_inc(conv_0, 1)
                    if h == TANH[n]:
                        act.wait_ge(conv_tap, 9 * g + 3 * (n + 1))
                        src, th = (qnT, vbT) if n == ITEM_Q else (cT[:], zs[:])
                        A(th, src, ACT.Tanh, scale=0.5).then_inc(tanh_done, 1)
                for n, dst, dst3 in ((ITEM_K, kn, kn3), (ITEM_Q, qn, qn3)):
                    if h == BACK[n]:
                        act.wait_ge(back_T, 3 * g + (n + 1))
                        for u in range(U):
                            ins = A(dst3[:, u], J[:, BANK[n] + u // HG, (u % HG) * P:(u % HG + 1) * P], ACT.Square,
                                    accum_out=rg[:, 0 if n == ITEM_K else 1, u:u + 1])
                        ins.then_inc(nsq_done, 1)
                    if h == NORM[n]:
                        act.wait_ge(nr_done, 2 * g + (n + 1))
                        for u in range(U):
                            ins = A(dst3[:, u], J[:, BANK[n] + u // HG, (u % HG) * P:(u % HG + 1) * P], ACT.Copy,
                                    scale=rg[:, n, u:u + 1])
                        ins.then_inc(norm_done, 1)
                if h == TK:
                    act.wait_ge(qk_T, 2 * g + 1)
                    dst = kq[:, :, 0:T].rearrange("p h (a c) -> p h a c", a=4)[:, :, 0:4:3]
                    A(dst, J[:, 0].rearrange("p (h a c) -> p h a c", h=HG, a=2), ACT.Copy).then_inc(kq_a, 1)
                if h == TQ:
                    act.wait_ge(qk_T, 2 * g + 2)
                    for t in range(NT):
                        ins = A(kq[:, :, t * T + C:t * T + C + P], J[:, 2 + t].rearrange("p (h t) -> p h t", h=HG), ACT.Copy)
                    ins.then_inc(kq_a, 1)
                if h == ROWS:
                    act.wait_ge(arg_done, g + 1)
                    A(mat(M_X), mat(M_X), ACT.Exp)
                    A(mat(M_U), mat(M_U), ACT.Exp, scale=-1.0)
                    A(mat(M_B0), J[:, 3].rearrange("p (u c) -> p u c", u=U), ACT.Copy).then_inc(exp_done, 1)
                for lv in range(LEVELS):
                    if h == INV + 3 * lv:
                        act.wait_ge(vpass, LEVELS * g + (lv + 1))
                        A(mat(M_V), J[:, 0].rearrange("p (u c) -> p u c", u=U), ACT.Copy).then_inc(vcopy, 1)
                if h == QTM:
                    act.wait_ge(qt_done, g + 1)
                    for ck in range(2):
                        r = slice(ck * C, ck * C + C)
                        ins = A(solve[r, :, 1 - ck], J[r, 3].rearrange("p (u c) -> p u c", u=U), ACT.Copy)
                    ins.then_inc(qt_copied, 1)
                for c in range(NCH):
                    if h == P2[c]:
                        act.wait_ge(p2_done, NCH * g + (c + 1))
                        A(VO, J[:, 1], ACT.Copy).then_inc(vo_done, 1)
                for t in range(NT):
                    if h == P2[2 * t + 1] + 1:
                        act.wait_ge(o_done, NCH * g + (2 * t + 2))
                        for u in range(t * HG, (t + 1) * HG):
                            ins = A(cT2[:, u * P:(u + 1) * P], qn3[:, u], ACT.Square, accum_out=rg[:, 2, u:u + 1])
                        ins.then_inc(osq_done, 1)
                if h == OT:
                    for b in range(2):
                        act.wait_ge(og_f, 2 * g + (3 + b))
                        A(og_hi[:, bass.ds(g * HG + 2 * b, 2), :], cT[:, 2 * b:2 * b + 2], ACT.Copy).then_inc(og_hi_done, 1)

            def swa_step(h, j):
                if h == 0:
                    act.wait_ge(sq_d, 4)
                    act.wait_ge(sq_a, 4)
                    A(qfix[:], xres[:, :, bass.ds(j * NB, NB)], ACT.Copy).then_inc(qfix_done, 1)
                if h == 3:
                    act.wait_ge(q_T, j + 1)
                    A(qTs[:, 0:2], J[:, 0].rearrange("p (a t) -> p a t", a=2), ACT.Copy).then_inc(qT_a, 1)
                for s in range(HQ):
                    pb = s % 2
                    if h == SCORE[s]:
                        act.wait_ge(negm_done, HQ * j + (s + 1))
                        if s >= 2:
                            act.wait_ge(p_T, HQ * j + (s - 1))
                        A(prob[:, pb, 0:P], sbuf_s[:, pb, 0:P], ACT.Exp, bias=negm[:, s, 0:1], accum_out=lsum[:, s, 0:1])
                        A(prob[:, pb, P:3 * P], sbuf_s[:, pb, P:3 * P], ACT.Exp, bias=negm[:, s, 1:2],
                          accum_out=lsum[:, s, 1:2])
                        A(esink[:, s], negm[:, s], ACT.Exp, bias=slf[:, 1, s:s + 1]).then_inc(exps_done, 1)
                    if h == PTURN[s]:
                        act.wait_ge(p_T, HQ * j + (s + 1))
                        A(probT[:, pb], J[:, 2, 0:3 * P], ACT.Copy).then_inc(pT_copied, 1)
                if h == 31:
                    act.wait_ge(oS_T, j + 1)
                    for b in range(2):
                        ins = A(os_hi[:, bass.ds(j * 4 + 2 * b, 2), :], J[:, b].rearrange("p (a t) -> p a t", a=2), ACT.Copy)
                    ins.then_inc(os_hi_done, 1)

            for i in range(4):
                act.wait_ge(x_in[i], 16)
                squares(i, nat1)
            act.wait_ge(ssq_x, 4)
            norm_rows(0, nat1)
            act.wait_ge(params_in, 64)
            for k in range(AHEAD):
                turn(0, k)
                split(0, k)
            tb, e, l, ea = ba[:, 64:96], ba[:, 128:160], ba[:, 160:192], ba[:, 192:224]
            ba3 = ba[:, 0:64].rearrange("p (t b h) -> p t b h", t=NT, b=2)

            def decay_step(h):
                if h == 12:
                    A(wba_hi[:], w_ba_sb, ACT.Copy).then_inc(wba_ready, 1)
                if h == 18:
                    act.wait_ge(ba_link, 1)
                    A(tb.rearrange("p (t h) -> p t h", t=NT), ba3[:, :, 0], ACT.Tanh, scale=0.5)
                    A(ea, a_log, ACT.Exp).then_inc(ba_act, 1)
                    act.wait_ge(ba_link, 2)
                    A(e, ba[:, 96:128], ACT.Abs).then_inc(ba_act, 1)
                    act.wait_ge(ba_act, 2)
                    A(e, e, ACT.Exp, scale=-1.0).then_inc(ba_act, 1)
                    act.wait_ge(ba_act, 3)
                    A(l, e, ACT.Ln, bias=1.0).then_inc(ba_act, 1)
                if h == 32:
                    act.wait_ge(decay_done, 1)
                    fl = lambda k: sc[:, k].rearrange("p t h -> p (t h)")
                    A(fl(K_OUT), J[:, 1, 0:32], ACT.Exp)
                    A(fl(DCOL), J[:, 1, 0:32], ACT.Copy)
                    A(fl(Q_OUT), J[:, 1, 64:96], ACT.Exp)
                    A(sc[:, CHDEC0:CHDEC1 + 1].rearrange("p c t h -> p (c t h)"), J[:, 1, 96:160], ACT.Exp).then_inc(ba_act, 1)
                    act.wait_ge(ba_link, 6)
                    A(fl(K_DEC), fl(K_DEC), ACT.Exp).then_inc(ba_act, 1)

            def read(q_end, ops):
                def f():
                    act.wait_ge(chunk_used, RING * q_end)
                    ops()
                return f

            def window(q0, jobs):
                for n in range(4):
                    def ops(n=n):
                        A(rawg[:, n, 0], acc[:, n % 2, 0], ACT.Copy).then_inc(rawg_a, 1)
                    output(q0 + n * (CPO // RING), jobs, read(q0 + (n + 1) * (CPO // RING), ops), h0=16 * n,
                           turned=0 if isinstance(q0, int) and n == 0 else None)

            window(0, decay_step)
            with act.Fori(1, NG) as w:
                window(w * CPO, lambda h: gdn_step(h, w - 1))

            def kv_step(h):
                gdn_step(h, NG - 1)
                if h == 66:
                    act.wait_ge(kv_T, 1)
                    for b in range(2):
                        ins = A(kT[:, 2 * b:2 * b + 2], J[:, 2 + b].rearrange("p (a t) -> p a t", a=2), ACT.Copy)
                    ins.then_inc(kT_done, 1)

            for n in range(5):
                def ops(n=n):
                    if n == 0:
                        act.wait_ge(front_T, 4 * NG - 3)
                        A(kdup[:, 0].rearrange("p (k d c) -> p k d c", k=4, d=2),
                          acc[:, 0, 0, 0:T].rearrange("p (k c) -> p k c", k=4).unsqueeze(2).broadcast_to([P, 4, 2, C]), ACT.Copy)
                        A(vs[:, 0], acc[:, 0, 0, T:2 * T], ACT.Copy).then_inc(kv_a, 1)
                    else:
                        A(xres[:, 0, (n - 1) * NB:n * NB], acc[:, n % 2, 0], ACT.Copy, scale=0.125).then_inc(sq_a, 1)
                q = (OUT_SWA + n) * (CPO // RING)
                output(q, kv_step, read(q + CPO // RING, ops), h0=16 * n)

            def gate(par, k):
                def ops():
                    if not isinstance(k, int) or k > 0:
                        act.wait_ge(merged, k)
                    for t in range(NT):
                        ins = A(gb[:, t], acc[:, par, t], ACT.Tanh, scale=0.5)
                    ins.then_inc(gate_done, 1)
                return ops

            act.wait_ge(og_lo_done, 2 * NG)
            def mix1(j):
                q = j * 4 + OUT_MIX1 * 2
                output(q, lambda h: swa_step(h, j), read(q + 2, gate(1, j)), h0=0)
                output(q + 2, lambda h: swa_step(h, j), lambda: None, h0=16)

            mix1(0)
            with act.Fori(1, 4) as j:
                mix1(j)
            with act.Fori(0, 4) as j:
                q = j * 4 + OUT_MIX2 * 2
                output(q, None, read(q + 2, gate(1, j + 4)))
                output(q + 2, None, lambda: None)
            for k in range(AHEAD):
                turn(1, k)
            def add_squares(n, first):
                def job(h):
                    if h == 4 and n:
                        act.wait_ge(x_added, first + n)
                        squares(n - 1, nat)
                return job

            act.wait_ge(merged, 8)
            for i in range(4):
                output((OUT_WO + i) * 2, add_squares(i, 0), lambda: None, turned=1 if i == 0 else None)
            act.wait_ge(x_added, 4)
            squares(3, nat)
            norm_rows(1, nat)
            for k in range(AHEAD):
                turn(2, k)

            def relu(p, par, k, skip):
                def ops():
                    if not skip:
                        act.wait_ge(up_T, k)
                    for t in range(NT):
                        ins = A(rbuf[:, p, t], acc[:, par, t], ACT.Relu)
                    ins.then_inc(relu_done, 1)
                return ops

            def up_job(b0, kt, cnt):
                def job(h):
                    if h == 2:
                        act.wait_ge(up_T, cnt)
                        for b in range(2):
                            ins = A(act_hi[:, bass.ds(kt + 2 * b, 2), :], J[:, b0 + b].rearrange("p (a t) -> p a t", a=2), ACT.Copy)
                        ins.then_inc(act_hi_done, 1)
                return job

            for hf in range(2):
                q0, r0 = (CH_FF + hf * CH_HALF) // RING, FF_UP * hf
                for p in range(2):
                    output(q0 + 2 * p, up_job(0, 0, r0 + 1) if p else None,
                           read(q0 + 2 * p + 2, relu(p, 1 - p, r0 + p - 1, r0 + p < 2)),
                           turned=2 if r0 + p == 0 else None)
                with act.Fori(1, FF_UP // 2) as i:
                    for p in range(2):
                        q = i * 4 + (q0 + 2 * p)
                        output(q, up_job(2 * (1 - p), i * 8 + 4 * (p - 1), i * 2 + (r0 + p)),
                               read(q + 2, relu(p, 1 - p, i * 2 + (r0 + p - 1), False)))
                qd = q0 + FF_UP * 2
                for n in range(FF_DOWN):
                    job = up_job(2, 28, r0 + FF_UP) if n == 0 else add_squares(n, 8) if hf == 1 else None
                    output(qd + 4 * n, job, lambda: None, nch=2 * CPO)
            act.wait_ge(x_added, 12)
            squares(3, nat)

        @block.vector
        def _(dve):
            V = nc.vector
            tt, ts, stt = V.tensor_tensor, V.tensor_scalar, V.scalar_tensor_tensor

            def split(q, k):
                slot = k % RING
                if isinstance(q, int) and RING * q + k >= N_CHUNKS:
                    return
                dve.wait_ge(hi_ready, RING * q + (k + 1))
                tt(w_lo[:, slot], raw[:, slot], w_hi[:, slot].bitcast(F32), ALU.subtract).then_inc(lo_ready, 1)

            def output(q0, jobs, epilogue, nch=CPO, h0=0, turned=None):
                for c in range(nch):
                    split(q0, c + AHEAD)
                    if turned is not None and c + 3 < CPO:
                        turn(turned, c + 3)
                    for k in range(CK):
                        if jobs:
                            jobs(h0 + c * CK + k)
                epilogue()

            def turn(k, i):
                hi, lo = (og_hi, og_lo) if k == 1 else (hT_hi, hT_lo)
                dve.wait_ge(turn_hi, 8 * k + i + 1)
                for kk in range(2):
                    kt = 2 * i + kk
                    ins = stt(out=lo[:, kt, :], in0=J[:, i % 4, kk * T:(kk + 1) * T],
                              scalar=0.5 if k == 1 else gain_cols[k][:, kt:kt + 1],
                              in1=hi[:, kt, :].bitcast(F32), op0=ALU.mult, op1=ALU.subtract)
                ins.then_inc(turn_lo, 1)

            def gdn_step(h, g):
                if h == 0:
                    dve.wait_ge(sc_ready, 1)
                    dve.wait_ge(ba_act, 6)
                    V.tensor_copy(scg[:].rearrange("p k t h -> p (k t) h"),
                                  sc[:].rearrange("p k t h -> p (k t) h")[:, :, bass.ds(g * HG, HG)])
                    V.tensor_copy(cwg[:], conv_w[:, :, bass.ds(g * HG, HG), :]).then_inc(par_ready, 1)
                if h == FRONT[ITEM_Z] + 1:
                    dve.wait_ge(tanh_done, 4 * g + 4)
                    for b in range(2):
                        zb = zs[:, 2 * b:2 * b + 2].rearrange("p a t -> p (a t)")
                        ins = stt(out=zb, in0=zb, scalar=1.0, in1=J[:, 2 + b], op0=ALU.add, op1=ALU.mult)
                    ins.then_inc(silu_done, 1)
                for i, n, dst in ((0, ITEM_K, kn3), (1, ITEM_Q, qn3)):
                    if h == BACK[n] + 1:
                        dve.wait_ge(nsq_done, 2 * g + (i + 1))
                        f = (1.0, float(P))[i]
                        ts(rg[:, i], rg[:, i], f, 4 * EPS * f, ALU.mult, ALU.add).then_inc(nssq_done, 1)
                for n in (ITEM_K, ITEM_Q, ITEM_V):
                    for s in (1, 2, 3):
                        if h == TAPS[n][s - 1]:
                            if s == 1:
                                dve.wait_ge(conv_0, 3 * g + (n + 1))
                            else:
                                dve.wait_ge(conv_tap, 9 * g + (3 * n + s - 1))
                            dst = qnT if n == ITEM_Q else cT
                            for m in range(HG):
                                b, o = BANK[n] + m // 2, (m % 2) * T
                                ins = stt(out=dst[:, m, s:T], in0=J[:, b, o:o + T - s], scalar=cwg[:, n, m, 3 - s:4 - s],
                                          in1=dst[:, m, s:T], op0=ALU.mult, op1=ALU.add)
                            ins.then_inc(conv_tap, 1)
                    if h == SILU[n]:
                        dve.wait_ge(tanh_done, 4 * g + (n + 1))
                        dst, th = (qnT, vbT) if n == ITEM_Q else (cT[:], zs[:])
                        stt(out=dst, in0=th, scalar=1.0, in1=dst, op0=ALU.add, op1=ALU.mult).then_inc(silu_done, 1)
                if h == BACK[ITEM_V] + 1:
                    dve.wait_ge(back_T, 3 * g + 3)
                    for t in range(NT):
                        ins = tt(vb3[:, t * HG:(t + 1) * HG], J[:, 2 + t].rearrange("p (h e) -> p h e", h=HG),
                                 wide(scu(BHALF)[:, t * HG:(t + 1) * HG], P), ALU.mult)
                    ins.then_inc(vb_done, 1)
                if h == ROWS:
                    dve.wait_ge(rows_done, g + 1)
                    tt(mat(M_V), J[:, 2].rearrange("p (u c) -> p u c", u=U), wide(scu(DCOL), C), ALU.subtract).then_inc(x0_link, 1)
                    dve.wait_ge(x0_link, g + 1)
                    ts(mat(M_X), mat(M_V), 0.0, None, ALU.min)
                    ts(mat(M_U), mat(M_V), 0.0, None, ALU.max).then_inc(arg_done, 1)
                if h == TK:
                    dve.wait_ge(qk_T, 2 * g + 1)
                    dst = kq[:, :, T:2 * T].rearrange("p h (a c) -> p h a c", a=4)[:, :, 0:4:3]
                    V.tensor_copy(dst, J[:, 1].rearrange("p (h a c) -> p h a c", h=HG, a=2)).then_inc(kq_d, 1)
                if h == KKQ:
                    dve.wait_ge(kkq_done, g + 1)
                    dve.wait_ge(mask_done, 5 * g + 5)
                    kk, kqp = (J[:, b].rearrange("p (u c) -> p u c", u=U) for b in (2, 3))
                    tt(mat(M_V), kk, mat(M_V), ALU.mult)
                    tt(mat(M_AT), kk, mat(M_B1), ALU.mult)
                    tt(mat(M_KQ), kqp, mat(M_KQ), ALU.mult).then_inc(at_ready, 1)
                if h == KKQ + 1:
                    dve.wait_ge(at_ready, g + 1)
                    tt(mat(M_U), mat(M_AT), over(nup1, U), ALU.mult).then_inc(u0_ready, 1)
                    dve.wait_ge(u0_ready, 2 * g + 1)
                    tt(mat(M_U), mat(M_U), over(eye64, U), ALU.add).then_inc(u0_ready, 1)
                for lv in range(LEVELS):
                    if h == INV + 3 * lv + 1:
                        dve.wait_ge(zpass, LEVELS * g + (lv + 1))
                        tt(mat(M_X), mat(M_X), J[:, 1].rearrange("p (u c) -> p u c", u=U), ALU.subtract)
                        z = J[:, 0].rearrange("p (u c) -> p u c", u=U)
                        if lv < LEVELS - 1:
                            tt(mat(M_U), mat(M_U), z, ALU.subtract).then_inc(inv_done, 1)
                            continue
                        for ck in range(2):
                            r = slice(ck * C, ck * C + C)
                            ins = tt(solve[r, :, ck], mats[r, M_U], z[r], ALU.subtract)
                        ins.then_inc(inv_done, 1)
                        V.memset(S[:], 0.0).then_inc(s_ready, 1)
                for c in range(NCH):
                    t, ck = divmod(c, 2)
                    kr, qr = slice(ck * C, ck * C + C), slice((1 - ck) * C, (2 - ck) * C)
                    if h == P1[c]:
                        dve.wait_ge(p1_done, NCH * g + (c + 1))
                        if c == 0:
                            dve.wait_ge(vb_done, g + 1)
                        for hd in range(HG):
                            ins = stt(out=RH[kr, hd * P:(hd + 1) * P], in0=J[kr, 0, hd * P:(hd + 1) * P],
                                      scalar=scg[kr, K_OUT, t, hd:hd + 1], in1=vb[kr, t, hd * P:(hd + 1) * P],
                                      op0=ALU.mult, op1=ALU.add)
                        ins.then_inc(rh_done, 1)
                    if h == P2[c]:
                        dve.wait_ge(vo_done, NCH * g + (c + 1))
                        for hd in range(HG):
                            ins = stt(out=qn[qr, t, hd * P:(hd + 1) * P], in0=J[qr, 0, hd * P:(hd + 1) * P],
                                      scalar=scg[qr, Q_OUT, t, hd:hd + 1], in1=VO[qr, hd * P:(hd + 1) * P],
                                      op0=ALU.mult, op1=ALU.add)
                        ins.then_inc(o_done, 1)
                    if h == P3[c]:
                        dve.wait_ge(p3_done, 3 * g + (c + 1))
                        dve.wait_ge(s_ready, NCH * g + (c + 1))
                        for hd in range(HG):
                            ins = stt(out=S[:, hd], in0=S[:, hd], scalar=scg[:, CHDEC0 + ck, t, hd:hd + 1],
                                      in1=J[:, 2, hd * P:(hd + 1) * P], op0=ALU.mult, op1=ALU.add)
                        ins.then_inc(s_ready, 1)
                if h == P2[-1] + 2:
                    dve.wait_ge(osq_done, 2 * g + 2)
                    ts(rg[:, 2], rg[:, 2], 4.0 / P, 4 * EPS, ALU.mult, ALU.add).then_inc(ossq_done, 1)
                if h == P2[-1] + 4:
                    dve.wait_ge(or_done, g + 1)
                    tt(qn3, qn3, wide(rg[:, 2], P), ALU.mult).then_inc(on_done, 1)
                if h == OT:
                    dve.wait_ge(o_T, g + 1)
                    for b in range(2):
                        src = J[:, b].rearrange("p (u a c) -> p u a c", u=4, a=2)
                        zz = zs[:, 2 * b:2 * b + 2].rearrange("p h (t a c) -> p (h t) a c", t=NT, a=2)
                        oo = cT[:, 2 * b:2 * b + 2].rearrange("p h (t a c) -> p (h t) a c", t=NT, a=2)
                        for a in range(2):
                            ins = stt(out=oo[:, :, a], in0=src[:, :, 1 - a], scalar=gdn_gain, in1=zz[:, :, a],
                                      op0=ALU.mult, op1=ALU.mult)
                        ins.then_inc(og_f, 1)
                    for b in range(2):
                        dve.wait_ge(og_hi_done, 2 * g + (b + 1))
                        heads = bass.ds(g * HG + 2 * b, 2)
                        tt(og_lo[:, heads, :], cT[:, 2 * b:2 * b + 2], og_hi[:, heads, :].bitcast(F32),
                           ALU.subtract).then_inc(og_lo_done, 1)

            def swa_step(h, j):
                if h == 0:
                    dve.wait_ge(kT_done, 1)
                    dve.wait_ge(kv_d, 1)
                    V.tensor_copy(kfix[:], kT[:, bass.ds(j, 1), :].rearrange("p a t -> p (a t)"))
                    V.tensor_copy(vfix[:], vs[:, :, bass.ds(j * C, C)])
                    V.tensor_copy(slf[:], rowp[:, 64:128].rearrange("p (a n) -> p a n", a=2)[:, :, bass.ds(j * HQ, HQ)]).then_inc(fix_done, 1)
                if h == 3:
                    dve.wait_ge(q_T, j + 1)
                    V.tensor_copy(qTs[:, 2:4], J[:, 1].rearrange("p (a t) -> p a t", a=2)).then_inc(qT_d, 1)
                for s in range(HQ):
                    pb = s % 2
                    if h == SCORE[s]:
                        dve.wait_ge(score_done, HQ * j + (s + 1))
                        if s == 0:
                            dve.wait_ge(fix_done, j + 1)
                            dve.wait_ge(dist_in, 16)
                        if s >= 2:
                            dve.wait_ge(exps_done, HQ * j + (s - 1))
                        stt(out=sbuf_s[:, pb], in0=dist[:], scalar=slf[:, 0, s:s + 1], in1=J[:, pb, 0:3 * P],
                            op0=ALU.mult, op1=ALU.add).then_inc(bias_done, 1)
                        dve.wait_ge(bias_done, HQ * j + (s + 1))
                        V.tensor_reduce(r3[:, s], sbuf_s[:, pb].rearrange("p (a k) -> p a k", a=3), AX_X, ALU.max).then_inc(max_link, 1)
                        dve.wait_ge(max_link, j * (2 * HQ) + (2 * s + 1))
                        tt(r3[:, s, 1:2], r3[:, s, 1:2], r3[:, s, 2:3], ALU.max).then_inc(max_link, 1)
                        dve.wait_ge(max_link, j * (2 * HQ) + (2 * s + 2))
                        ts(negm[:, s], r3[:, s, 0:2], slf[:, 1, s:s + 1], -1.0, ALU.max, ALU.mult).then_inc(negm_done, 1)
                    if h == PV[s] and s % 2:
                        i, pair = s // 2, slice(s - 1, s + 1)
                        dve.wait_ge(pv_done, HQ * j + (s + 1))
                        tt(lsum[:, pair], lsum[:, pair], esink[:, pair], ALU.add).then_inc(l_link, 1)
                        dve.wait_ge(l_link, j * HQ + (2 * i + 1))
                        V.reciprocal(lsum[:, pair], lsum[:, pair]).then_inc(l_link, 1)
                        dve.wait_ge(l_link, j * HQ + (2 * i + 2))
                        tt(oS[:, :, (s - 1) * C:(s + 1) * C].rearrange("p t (s c) -> p s t c", s=2),
                           J[:, 3, (s - 1) % 4 * P:((s - 1) % 4 + 2) * P].rearrange("p (s t c) -> p s t c", s=2, t=NT),
                           lsum[:, pair].unsqueeze(3).broadcast_to([P, 2, NT, C]), ALU.mult).then_inc(oS_done, 1)
                if h == 31:
                    dve.wait_ge(os_hi_done, j + 1)
                    for b in range(2):
                        ins = tt(os_lo[:, bass.ds(j * 4 + 2 * b, 2), :], J[:, b].rearrange("p (a t) -> p a t", a=2),
                                 os_hi[:, bass.ds(j * 4 + 2 * b, 2), :].bitcast(F32), ALU.subtract)
                    ins.then_inc(os_lo_done, 1)

            def norm_rows(k, dst):
                dve.wait_ge(ssq_x, 4 * k + 4)
                V.tensor_reduce(stat[:, 0:2], part[:], AX_X, ALU.add).then_inc(sum_link, 1)
                dve.wait_ge(sum_link, k + 1)
                ts(stat[:, 0:2], stat[:, 0:2], 1.0 / D, EPS, ALU.mult, ALU.add).then_inc(sum_ready, 1)
                dve.wait_ge(r_x, k + 1)
                if dst is None:
                    return
                for i in range(4):
                    w = slice(i * NB, (i + 1) * NB)
                    ts(dst[:, 1, w], xres[:, 1, w], stat[:, 3:4], None, ALU.mult).then_inc(nat_d, 1)

            norm_rows(0, nat1)
            for k in range(AHEAD):
                turn(0, k)
                split(0, k)
            flat = lambda k: sc[:, k].rearrange("p t h -> p (t h)")
            ba3 = ba[:, 0:64].rearrange("p (t b h) -> p t b h", t=NT, b=2)
            tb, a2, l, ea, mx = (ba[:, o:o + 32] for o in (64, 96, 160, 192, 224))
            def decay_step(h):
                if h == 12:
                    dve.wait_ge(wba_ready, 1)
                    tt(wba_lo[:], w_ba_sb, wba_hi[:].bitcast(F32), ALU.subtract).then_inc(wba_ready, 1)
                if h == 18:
                    dve.wait_ge(ba_done, 1)
                    V.tensor_copy(ba[:, 0:64], J[:, 0, 0:64]).then_inc(ba_link, 1)
                    dve.wait_ge(ba_link, 1)
                    tt(a2.rearrange("p (t h) -> p t h", t=NT), ba3[:, :, 1], dt_bias.rearrange("p (t h) -> p t h", t=NT),
                       ALU.add).then_inc(ba_link, 1)
                    dve.wait_ge(ba_link, 2)
                    ts(mx, a2, 0.0, None, ALU.max).then_inc(ba_link, 1)
                    dve.wait_ge(ba_act, 4)
                    dve.wait_ge(ba_link, 3)
                    tt(mx, mx, l, ALU.add).then_inc(ba_link, 1)
                    dve.wait_ge(ba_link, 4)
                    stt(out=flat(G), in0=mx, scalar=-1.0, in1=ea, op0=ALU.mult, op1=ALU.mult).then_inc(g_ready, 1)
                    ts(flat(BETA), tb, 0.5, 0.5, ALU.mult, ALU.add)
                    ts(flat(BHALF), tb, 0.25, 0.25, ALU.mult, ALU.add).then_inc(ba_link, 1)
                    dve.wait_ge(g_ready, 1)
                    for ck in range(2):
                        ts(flat(CHDEC0 + ck), flat(G), chunk_sel[:, ck:ck + 1], None, ALU.mult).then_inc(g_ready, 1)
                if h == 32:
                    dve.wait_ge(ba_act, 5)
                    dve.wait_ge(ba_link, 5)
                    tt(flat(K_DEC), J[:, 1, 32:64], flat(DCOL), ALU.subtract).then_inc(ba_link, 1)
                    V.memset(S[:], 0.0).then_inc(og_f, 2)
                    stt(out=flat(K_OUT), in0=flat(K_OUT), scalar=-1.0, in1=flat(BETA), op0=ALU.mult, op1=ALU.mult
                        ).then_inc(sc_ready, 1)

            def read(q_end, ops):
                def f():
                    dve.wait_ge(chunk_used, RING * q_end)
                    ops()
                return f

            def window(q0, jobs):
                for n in range(4):
                    def ops(n=n):
                        V.tensor_copy(rawg[:, n, 1], acc[:, n % 2, 1]).then_inc(rawg_d, 1)
                    output(q0 + n * (CPO // RING), jobs, read(q0 + (n + 1) * (CPO // RING), ops), h0=16 * n,
                           turned=0 if isinstance(q0, int) and n == 0 else None)

            window(0, decay_step)
            with dve.Fori(1, NG) as w:
                window(w * CPO, lambda h: gdn_step(h, w - 1))

            for n in range(5):
                def ops(n=n):
                    if n == 0:
                        dve.wait_ge(front_T, 4 * NG - 3)
                        V.tensor_copy(kdup[:, 1].rearrange("p (k d c) -> p k d c", k=4, d=2),
                                      acc[:, 0, 1, 0:T].rearrange("p (k c) -> p k c", k=4).unsqueeze(2).broadcast_to([P, 4, 2, C]))
                        V.tensor_copy(vs[:, 1], acc[:, 0, 1, T:2 * T]).then_inc(kv_d, 1)
                    else:
                        ts(xres[:, 1, (n - 1) * NB:n * NB], acc[:, n % 2, 1], 0.125, None, ALU.mult).then_inc(sq_d, 1)
                q = (OUT_SWA + n) * (CPO // RING)
                output(q, lambda h: gdn_step(h, NG - 1), read(q + CPO // RING, ops), h0=16 * n)

            with dve.Fori(0, 4) as j:
                q = j * 4 + OUT_MIX1 * 2

                def merge():
                    dve.wait_ge(gate_done, j + 1)
                    dve.wait_ge(qfix_done, j + 1)
                    for t in range(NT):
                        ins = stt(out=xres[:, t, bass.ds(j * NB, NB)], in0=gb[:, t], scalar=1.0, in1=acc[:, 0, t],
                                  op0=ALU.add, op1=ALU.mult)
                    ins.then_inc(merged, 1)
                output(q, lambda h: swa_step(h, j), lambda: None, h0=0)
                output(q + 2, lambda h: swa_step(h, j), read(q + 4, merge), h0=16)
            with dve.Fori(0, 4) as j:
                q = j * 4 + OUT_MIX2 * 2

                def merge():
                    dve.wait_ge(gate_done, j + 5)
                    for t in range(NT):
                        ins = stt(out=gb[:, t], in0=gb[:, t], scalar=1.0, in1=acc[:, 0, t], op0=ALU.add, op1=ALU.mult)
                    ins.then_inc(merge_link, 1)
                    dve.wait_ge(merge_link, j + 1)
                    dst = xres[:, :, bass.ds(j * NB, NB)]
                    tt(dst, dst, gb[:], ALU.add).then_inc(merged, 1)
                output(q, None, lambda: None)
                output(q + 2, None, read(q + 4, merge))
            for k in range(AHEAD):
                turn(1, k)

            def add_x(col, back=None):
                def make(par):
                    def ops():
                        if back is not None:
                            dve.wait_ge(x_back[back], 16)
                        for t in range(NT):
                            dst = xres[:, t, col]
                            ins = tt(dst, dst, acc[:, par, t], ALU.add)
                        ins.then_inc(x_added, 1)
                    return ops
                return make

            for i in range(4):
                q = (OUT_WO + i) * 2
                output(q, None, read(q + 2, add_x(slice(i * NB, (i + 1) * NB), i)(1 - i % 2)),
                       turned=1 if i == 0 else None)
            dve.wait_ge(x_added, 4)
            norm_rows(1, nat)
            for k in range(AHEAD):
                turn(2, k)

            def square(p, k):
                def ops():
                    dve.wait_ge(relu_done, k)
                    for t in range(NT):
                        ins = tt(rbuf[:, p, t], acc[:, 1 - p, t], rbuf[:, p, t], ALU.mult)
                    ins.then_inc(relu_sq, 1)
                return ops

            def up_job(b0, kt, cnt):
                def job(h):
                    if h == 2:
                        dve.wait_ge(act_hi_done, cnt)
                        for b in range(2):
                            ins = tt(act_lo[:, bass.ds(kt + 2 * b, 2), :], J[:, b0 + b].rearrange("p (a t) -> p a t", a=2),
                                     act_hi[:, bass.ds(kt + 2 * b, 2), :].bitcast(F32), ALU.subtract)
                        ins.then_inc(act_lo_done, 1)
                return job

            for hf in range(2):
                q0, r0 = (CH_FF + hf * CH_HALF) // RING, FF_UP * hf
                for p in range(2):
                    output(q0 + 2 * p, up_job(0, 0, r0 + 1) if p else None, read(q0 + 2 * p + 2, square(p, r0 + p + 1)),
                           turned=2 if r0 + p == 0 else None)
                with dve.Fori(1, FF_UP // 2) as i:
                    for p in range(2):
                        q = i * 4 + (q0 + 2 * p)
                        output(q, up_job(2 * (1 - p), i * 8 + 4 * (p - 1), i * 2 + (r0 + p)),
                               read(q + 2, square(p, i * 2 + (r0 + p + 1))))
                qd = q0 + FF_UP * 2
                for n in range(FF_DOWN):
                    output(qd + 4 * n, up_job(2, 28, r0 + FF_UP) if n == 0 else None,
                           read(qd + 4 * n + 4, add_x(slice(n * NB, (n + 1) * NB))(1 - n % 2)), nch=2 * CPO)
            norm_rows(2, None)
            dve.wait_ge(dist_in, 32)
            for i in range(4):
                w = slice(i * NB, (i + 1) * NB)
                for t in range(NT):
                    ins = stt(out=nat[:, t, w], in0=xres[:, t, w], scalar=stat[:, 2 + t:3 + t], in1=fgain[:, w],
                              op0=ALU.mult, op1=ALU.mult)
                ins.then_inc(y_ready, 1)

        @block.gpsimd
        def _(pool):
            tt, ts = nc.gpsimd.tensor_tensor, nc.gpsimd.tensor_scalar
            nc.gpsimd.memset(stat[:, 4:16], -0.5).then_inc(half_ready, 1)

            def row_factor(k):
                pool.wait_ge(sum_ready, k + 1)
                tt(stat[:, 2:4], stat[:, 0:2], stat[:, 4:6], ALU.pow).then_inc(r_x, 1)

            pool.wait_ge(half_ready, 1)
            row_factor(0)

            def group(g):
                def power(i, wait, value, done):
                    pool.wait_ge(wait, value)
                    tt(rg[:, i], rg[:, i], stat[:, 8:16], ALU.pow).then_inc(done, 1)

                pool.wait_ge(par_ready, g + 1)
                tt(mat(M_B0), wide(scu(G), C), over(tri64, U), ALU.mult).then_inc(rows_rhs, 1)
                tt(mat(M_B1), wide(scu(BETA), C), over(eye64, U), ALU.mult).then_inc(rows_rhs, 1)
                power(0, nssq_done, 2 * g + 1, nr_done)
                pool.wait_ge(exp_done, g + 1)
                tt(mat(M_KQ), mat(M_X), over(upi, U), ALU.mult).then_inc(mask_done, 1)
                tt(mat(M_B1), mat(M_X), mat(M_B0), ALU.mult).then_inc(mask_done, 1)
                pool.wait_ge(mask_done, 5 * g + 2)
                tt(mat(M_B1), mat(M_B1), over(up, U), ALU.mult).then_inc(mask_done, 1)
                tt(mat(M_V), mat(M_U), over(low, U), ALU.mult).then_inc(mask_done, 1)
                power(1, nssq_done, 2 * g + 2, nr_done)
                pool.wait_ge(mask_done, 5 * g + 4)
                tt(mat(M_V), mat(M_V), wide(scu(BETA), C), ALU.mult).then_inc(mask_done, 1)
                pool.wait_ge(at_ready, g + 1)
                tt(mat(M_X), mat(M_V), over(nlow1, U), ALU.mult).then_inc(xu_link, 1)
                tt(mat(M_B0), mat(M_AT), over(up_level[0], U), ALU.mult).then_inc(bt_ready, 1)
                pool.wait_ge(xu_link, g + 1)
                tt(mat(M_X), mat(M_X), over(eye64, U), ALU.add).then_inc(x0_ready, 1)
                for lv in range(1, LEVELS):
                    if lv >= 2:
                        pool.wait_ge(vpass, LEVELS * g + (lv - 1))
                    tt(mat(M_B0 + lv % 2), mat(M_AT), over(up_level[lv], U), ALU.mult).then_inc(bt_ready, 1)
                    if lv == 1:
                        pool.wait_ge(qk_T, 2 * g + 1)
                        tt(kn3, kn3, wide(scu(K_DEC), P), ALU.mult).then_inc(kdec_done, 1)
                power(2, ossq_done, g + 1, or_done)

            with pool.Fori(0, NG) as g:
                group(g)
            for b in range(4):
                pool.wait_ge(turn_T, CPO + 2 * b + 2)
                cols = slice(b * NB, (b + 1) * NB)
                pool.dma_start(xres[:, :, cols], x[:, :, cols]).then_inc(x_back[b], 16)
            row_factor(1)
            row_factor(2)


def program(nc, ap, outs):
    hybrid_trunk(nc, ap["x"].rearrange("(t p) d -> p t d", p=P), ap["weights"], ap["w_ba"], ap["colp"], ap["rowp"],
                 ap["masks"], ap["dist"], ap["fgain"], outs.rearrange("(t p) d -> p t d", p=P))


def mask_constants():
    p = np.arange(P)
    same = (p[:, None] // C) == (p[None, :] // C)
    tri = same & (p[:, None] <= p[None, :])
    r, j = (p % C)[:, None], np.arange(C)[None, :]
    small = [r <= j, r == j, r > j, r <= j, r < j]
    nlow1 = -((r // 2 == j // 2) & (r > j)).astype(np.float32)
    nup1 = -((r // 2 == j // 2) & (r < j)).astype(np.float32)
    levels = []
    for lv in range(LEVELS):
        s = 2 << lv
        levels.append((r // (2 * s) == j // (2 * s)) & ((j // s) % 2 == 1) & ((r // s) % 2 == 0))
    parts = [np.eye(P), tri, tri[:, p ^ C], same, np.ones((P, P)), *small, nlow1, nup1, *levels]
    return np.concatenate([np.asarray(a, np.float32) for a in parts], axis=1)


def distances():
    q, k = np.arange(P)[:, None], np.arange(P)[None, :]
    own = np.where(q >= k, k - q, NEG)
    prev = np.where(k > q, k - q - P, NEG)
    return np.concatenate([own, prev, own], axis=1).astype(np.float32)


def kernel(**inputs):
    import numpy as _np
    import concourse.bacc as _bacc
    from concourse import mybir as _mybir
    from concourse.bass_utils import run_bass_kernel_spmd as _run

    a = {k: _np.asarray(v) for k, v in inputs.items()}
    w_in = a["w_in"][0]
    W = 4 * D
    b0, sq0, sk0, sv0, gt0 = W, W + 32, W + 32 + D, W + 32 + D + 256, W + 32 + D + 512

    def chunks(w):
        return w.reshape(-1, CK, P, NB).transpose(0, 2, 1, 3).reshape(-1, P, CK * NB)

    stream = []
    for g in range(NG):
        for base in (D, 0, 2 * D, 3 * D):
            stream.append(chunks(w_in[:, base + g * NB:base + (g + 1) * NB]))
    stream.append(chunks(w_in[:, sk0:sk0 + NB]))
    for i in range(4):
        stream.append(chunks(w_in[:, sq0 + i * NB:sq0 + (i + 1) * NB]))
    for base, w in ((gt0, a["w_branch_gdn"][0]), (gt0 + D, a["w_branch_swa"][0])):
        for i in range(4):
            stream.append(chunks(w_in[:, base + i * NB:base + (i + 1) * NB]))
            stream.append(chunks(w[:, i * NB:(i + 1) * NB]))
    for i in range(4):
        stream.append(chunks(a["w_out"][0][:, i * NB:(i + 1) * NB]))
    for hf in range(2):
        for i in range(FF_UP):
            o = hf * (DFF // 2) + i * NB
            stream.append(chunks(a["w_ff_up"][0][:, o:o + NB]))
        for i in range(FF_DOWN):
            stream.append(chunks(a["w_ff_down"][0][hf * (DFF // 2):(hf + 1) * (DFF // 2), i * NB:(i + 1) * NB]))

    def column(v):
        return v.reshape(-1, P).T

    conv = a["conv_w"][0].reshape(4, 3, KT, P)[:, [1, 0, 2]].transpose(3, 1, 2, 0).reshape(P, 192)
    sel = _np.repeat(_np.eye(2, dtype=_np.float32), C, axis=0)
    slopes = (2.0 ** (-8.0 * _np.arange(1, 33) / 32)).astype(_np.float32)
    rows = [_np.tile(a["dt_bias"][0], 2), _np.tile(a["a_log"][0], 2), slopes, a["attn_sinks"][0]]
    arrays = {
        "x": a["x"][0],
        "weights": _np.concatenate(stream),
        "w_ba": w_in[:, b0:b0 + 32].reshape(KT, P, 32).transpose(1, 0, 2).reshape(P, 512),
        "colp": _np.concatenate([conv, column(a["norm1_g"][0]), column(a["norm2_g"][0]), column(a["gdn_norm_g"][0]), sel],
                                axis=1),
        "rowp": _np.tile(_np.concatenate(rows)[None, :], (P, 1)),
        "masks": mask_constants(),
        "dist": distances(),
        "fgain": _np.tile(a["final_norm_g"][None, :], (P, 1)),
    }
    nc = _bacc.Bacc("TRN2", target_bir_lowering=False, num_devices=1)
    arrays = {k: _np.ascontiguousarray(v) for k, v in arrays.items()}
    ap = {k: nc.dram_tensor(k, v.shape, _mybir.dt.from_np(v.dtype), kind="ExternalInput").ap() for k, v in arrays.items()}
    y = nc.dram_tensor("y", (T, D), F32, kind="ExternalOutput").ap()
    program(nc, ap, y)
    r = _run(nc, [arrays], core_ids=[0])
    return r.results[0]["y"].reshape(1, T, D)
```
